# Optimizing a Trainium2 kernel written in Bass

```python
import math
import jax, jax.numpy as jnp
from jax import lax
import numpy as np

D_MODEL = 1024
BATCH = 1
SEQ = 256
DEPTH = 2

N_A_LAYERS = (DEPTH + 1) // 2
N_B_LAYERS = DEPTH - N_A_LAYERS

A_HEADS = 8
A_EXPAND = 128
A_FDIM = A_HEADS * A_EXPAND
A_VDIM = D_MODEL // A_HEADS
A_CHUNK = 32

B_HEADS = 8
B_HEAD_DIM = D_MODEL // B_HEADS // 2
B_VDIM = 2 * B_HEAD_DIM
B_QK_DIM = B_HEADS * 2 * B_HEAD_DIM
B_QBLOCK = 128

N_GROUPS = 4
EXPERTS_PER_GROUP = 8
N_EXPERTS = N_GROUPS * EXPERTS_PER_GROUP
TOP_K_INNER = 2
D_EXPERT = 512

NORM_EPS = 1e-6
SUBLN_EPS = 1e-5

kernel_name = "yoco_hgrn2_diffattn_hmoe"

def rmsnorm(x, g, eps=NORM_EPS):
    xf = x.astype(jnp.float32)
    y = xf * lax.rsqrt(jnp.mean(xf * xf, axis=-1, keepdims=True) + eps)
    return y.astype(x.dtype) * g

def gla_chunk(q, k, v, log_f):
    Bsz, S, H, K = q.shape
    V = v.shape[-1]
    N = S // A_CHUNK

    def to_chunks(t):
        return t.reshape(Bsz, N, A_CHUNK, H, t.shape[-1]).transpose(1, 0, 3, 2, 4)

    qc, kc, vc, bc = to_chunks(q), to_chunks(k), to_chunks(v), to_chunks(log_f)
    bc = jnp.cumsum(bc, axis=-2)
    causal = jnp.tril(jnp.ones((A_CHUNK, A_CHUNK), dtype=bool))

    def step(state, inp):
        qn, kn, vn, bn = inp
        b_last = bn[..., -1:, :]
        q_dec = qn * jnp.exp(bn)
        k_inv = kn * jnp.exp(-bn)
        scores = jnp.where(causal, jnp.einsum('bhck,bhsk->bhcs', q_dec, k_inv), 0.0)
        o = (jnp.einsum('bhcs,bhsv->bhcv', scores, vn)
             + jnp.einsum('bhck,bhkv->bhcv', q_dec, state))
        k_to_end = kn * jnp.exp(b_last - bn)
        state = (jnp.exp(b_last)[..., 0, :, None] * state
                 + jnp.einsum('bhck,bhcv->bhkv', k_to_end, vn))
        return state, o

    s0 = jnp.zeros((Bsz, H, K, V), jnp.float32)
    _, o = lax.scan(step, s0, (qc, kc, vc, bc))
    return o.transpose(1, 0, 3, 2, 4).reshape(Bsz, S, H, V)

def hgrn2_mixer(h, w_in, lb, onorm_g, w_out):
    Bsz, S, _ = h.shape
    proj = h @ w_in
    q, fz, i_in, g = jnp.split(proj, [A_FDIM, 2 * A_FDIM, 2 * A_FDIM + D_MODEL], axis=-1)
    q = jax.nn.silu(q.astype(jnp.float32))
    fz = fz.astype(jnp.float32)
    lb32 = lb.astype(jnp.float32)
    log_f = jnp.log(lb32 + (1.0 - lb32) * jax.nn.sigmoid(fz))
    k = (1.0 - lb32) * jax.nn.sigmoid(-fz)
    o = gla_chunk(q.reshape(Bsz, S, A_HEADS, A_EXPAND),
                  k.reshape(Bsz, S, A_HEADS, A_EXPAND),
                  i_in.astype(jnp.float32).reshape(Bsz, S, A_HEADS, A_VDIM),
                  log_f.reshape(Bsz, S, A_HEADS, A_EXPAND))
    gate = jax.nn.silu(g.reshape(Bsz, S, A_HEADS, A_VDIM))
    o = (rmsnorm(o, onorm_g) * gate).astype(h.dtype)
    return o.reshape(Bsz, S, D_MODEL) @ w_out

def shared_kv(h, kv_norm_g, w_kv):
    Bsz, S, _ = h.shape
    kv = rmsnorm(h, kv_norm_g) @ w_kv
    k_all, v_all = jnp.split(kv, [B_QK_DIM], axis=-1)
    k_sh = k_all.reshape(Bsz, S, B_HEADS, 2, B_HEAD_DIM).transpose(3, 0, 2, 1, 4)
    v_sh = v_all.reshape(Bsz, S, B_HEADS, B_VDIM).transpose(0, 2, 1, 3)
    return k_sh, v_sh

def diff_attention(h, k_sh, v_sh, w_q, lam, subln_g, w_out, lambda_init):
    Bsz, S, _ = h.shape
    q = (h @ w_q).reshape(Bsz, S, B_HEADS, 2, B_HEAD_DIM)
    lam32 = lam.astype(jnp.float32)
    lam_full = (jnp.exp(jnp.sum(lam32[0] * lam32[1])) - jnp.exp(jnp.sum(lam32[2] * lam32[3]))
                + lambda_init)
    nb = S // B_QBLOCK
    qb = q.reshape(Bsz, nb, B_QBLOCK, B_HEADS, 2, B_HEAD_DIM).transpose(1, 4, 0, 3, 2, 5)
    key_pos = jnp.arange(S)
    scale = B_HEAD_DIM ** -0.5

    def block(args):
        qblk, bi = args
        q_pos = bi * B_QBLOCK + jnp.arange(B_QBLOCK)
        mask = key_pos[None, :] <= q_pos[:, None]
        s = jnp.einsum('mbhqd,mbhkd->mbhqk', qblk, k_sh).astype(jnp.float32) * scale
        p = jax.nn.softmax(jnp.where(mask, s, -jnp.inf), axis=-1)
        p = p[0] - lam_full * p[1]
        return jnp.einsum('bhqk,bhkv->bhqv', p.astype(v_sh.dtype), v_sh)

    o = lax.map(block, (qb, jnp.arange(nb)))
    o = o.transpose(1, 0, 3, 2, 4).reshape(Bsz, S, B_HEADS, B_VDIM)
    o = rmsnorm(o, subln_g, SUBLN_EPS) * (1.0 - lambda_init)
    return o.reshape(Bsz, S, D_MODEL).astype(h.dtype) @ w_out

def hier_moe(h, wg, bg, we, be, w_gu, w_down):
    Bsz, S, D = h.shape
    t = h.reshape(-1, D)
    T = t.shape[0]
    coarse = jax.nn.softmax((t @ wg + bg).astype(jnp.float32), axis=-1)
    grp = jnp.argmax(coarse, axis=-1)
    p_grp = jnp.take_along_axis(coarse, grp[:, None], axis=-1)
    fine = (t @ we + be).astype(jnp.float32).reshape(T, N_GROUPS, EXPERTS_PER_GROUP)
    fine = jnp.take_along_axis(fine, grp[:, None, None], axis=1)[:, 0]
    top_p, top_i = lax.top_k(jax.nn.softmax(fine, axis=-1), TOP_K_INNER)
    w = p_grp * top_p / jnp.sum(top_p, axis=-1, keepdims=True)
    eid = grp[:, None] * EXPERTS_PER_GROUP + top_i
    gates = jnp.sum(jax.nn.one_hot(eid, N_EXPERTS, dtype=jnp.float32) * w[..., None], axis=1)

    def expert(acc, inp):
        wgu, wd, g = inp
        a, u = jnp.split(t @ wgu, 2, axis=-1)
        y = (jax.nn.silu(a) * u) @ wd
        return acc + g[:, None].astype(y.dtype) * y, None

    out, _ = lax.scan(expert, jnp.zeros_like(t), (w_gu, w_down, gates.T))
    return out.reshape(Bsz, S, D)

def setup_inputs(seed: int = 0) -> dict:
    key = jax.random.key(seed)
    ks = jax.random.split(key, 24)

    def dense(k, shape, fan_in):
        return jax.random.normal(k, shape, jnp.float32) * (fan_in ** -0.5)

    def gain(k, shape):
        return 1.0 + 0.02 * jax.random.normal(k, shape, jnp.float32)

    return {
        "x": jax.random.normal(ks[0], (BATCH, SEQ, D_MODEL), jnp.float32),
        "a_norm_g": gain(ks[1], (N_A_LAYERS, D_MODEL)),
        "a_w_in": dense(ks[2], (N_A_LAYERS, D_MODEL, 2 * A_FDIM + 2 * D_MODEL), D_MODEL),
        "a_lb": 0.1 * jax.random.normal(ks[3], (N_A_LAYERS + 1, A_FDIM), jnp.float32),
        "a_onorm_g": gain(ks[4], (N_A_LAYERS, A_VDIM)),
        "a_w_out": dense(ks[5], (N_A_LAYERS, D_MODEL, D_MODEL), D_MODEL),
        "kv_norm_g": gain(ks[6], (D_MODEL,)),
        "w_kv": dense(ks[7], (D_MODEL, B_QK_DIM + B_HEADS * B_VDIM), D_MODEL),
        "b_norm_g": gain(ks[8], (N_B_LAYERS, D_MODEL)),
        "b_w_q": dense(ks[9], (N_B_LAYERS, D_MODEL, B_QK_DIM), D_MODEL),
        "b_lam": 0.1 * jax.random.normal(ks[10], (N_B_LAYERS, 4, B_HEAD_DIM), jnp.float32),
        "b_subln_g": gain(ks[11], (N_B_LAYERS, B_VDIM)),
        "b_w_out": dense(ks[12], (N_B_LAYERS, D_MODEL, D_MODEL), D_MODEL),
        "ffn_norm_g": gain(ks[13], (DEPTH, D_MODEL)),
        "router_g_w": dense(ks[14], (DEPTH, D_MODEL, N_GROUPS), D_MODEL),
        "router_g_b": 0.01 * jax.random.normal(ks[15], (DEPTH, N_GROUPS), jnp.float32),
        "router_e_w": dense(ks[16], (DEPTH, D_MODEL, N_EXPERTS), D_MODEL),
        "router_e_b": 0.01 * jax.random.normal(ks[17], (DEPTH, N_EXPERTS), jnp.float32),
        "expert_w_gu": dense(ks[18], (DEPTH, N_EXPERTS, D_MODEL, 2 * D_EXPERT), D_MODEL),
        "expert_w_down": dense(ks[19], (DEPTH, N_EXPERTS, D_EXPERT, D_MODEL), D_EXPERT),
        "final_norm_g": gain(ks[20], (D_MODEL,)),
    }

def reference(x, a_norm_g, a_w_in, a_lb, a_onorm_g, a_w_out, kv_norm_g, w_kv, b_norm_g, b_w_q,
              b_lam, b_subln_g, b_w_out, ffn_norm_g, router_g_w, router_g_b, router_e_w,
              router_e_b, expert_w_gu, expert_w_down, final_norm_g):
    lb_all = jnp.cumsum(jax.nn.softmax(a_lb.astype(jnp.float32), axis=0), axis=0)
    h = x
    k_sh = v_sh = None
    for layer in range(DEPTH):
        if layer < N_A_LAYERS:
            a = layer
            h = h + hgrn2_mixer(rmsnorm(h, a_norm_g[a]), a_w_in[a], lb_all[a],
                                a_onorm_g[a], a_w_out[a])
        else:
            if layer == N_A_LAYERS:
                k_sh, v_sh = shared_kv(h, kv_norm_g, w_kv)
            b = layer - N_A_LAYERS
            lambda_init = 0.8 - 0.6 * math.exp(-0.3 * layer)
            h = h + diff_attention(rmsnorm(h, b_norm_g[b]), k_sh, v_sh, b_w_q[b], b_lam[b],
                                   b_subln_g[b], b_w_out[b], lambda_init)
        h = h + hier_moe(rmsnorm(h, ffn_norm_g[layer]), router_g_w[layer], router_g_b[layer],
                         router_e_w[layer], router_e_b[layer], expert_w_gu[layer],
                         expert_w_down[layer])
    return rmsnorm(h, final_norm_g)


_drawn_inputs = setup_inputs


def setup_inputs(seed=0):
    import zlib

    import numpy as np

    out = dict(_drawn_inputs(seed))
    spreads = {}
    factors = {'router_g_b': 9.406, 'final_norm_g': 8.679, 'b_norm_g': 2.959}
    for name, (base, spread) in spreads.items():
        noise = np.random.default_rng([zlib.crc32(name.encode()), seed]).standard_normal(out[name].shape)
        drawn = base * np.exp(spread * noise) if base else spread * noise
        out[name] = __import__('jax').numpy.asarray(drawn.astype(out[name].dtype))
    for name, factor in factors.items():
        out[name] = (out[name] * factor).astype(out[name].dtype)
    return out
```

```python
import math
from contextlib import ExitStack

import concourse.bass as bass
from concourse import mybir

F32 = mybir.dt.float32
I32 = mybir.dt.int32
ALU = mybir.AluOpType
ACT = mybir.ActivationFunctionType
AX = mybir.AxisListType.X

P = 128
S, D = 256, 1024
TB = S // P
KC = D // P
HEADS = 8
CH, NCH = 32, 8
G4, E8 = 4, 8
NE = G4 * E8
LG = G4 + NE
DE = 512
CAP = 64
ROUNDS = S // CAP
NS = 9
GRP = 3
SW = 36
DH = 64
LAM_INIT = 0.8 - 0.6 * math.exp(-0.3)
FAR = 1.0e4
NEG = -1.0e30

GA_A, GA_LB, GA_KV, GA_B, GA_F, GA_ON, GA_SL, NG = 0, 8, 24, 32, 40, 56, 57, 58


class Chain:

    def __init__(self, engine, sem):
        self.engine, self.sem, self.n = engine, sem, 0

    def link(self, instruction):
        instruction.then_inc(self.sem, 1)
        self.n += 1
        self.engine.wait_ge(self.sem, self.n)


def trunk(nc, x, a_norm_g, a_w_in, a_lb, a_onorm_g, a_w_out, kv_norm_g, w_kv, b_norm_g, b_w_q, b_lam,
          b_subln_g, b_w_out, ffn_norm_g, router_g_w, router_g_b, router_e_w, router_e_b,
          expert_w_gu, expert_w_down, final_norm_g, out):
    ctx = ExitStack()
    with ctx:
        def sb(name, shape, dt=F32):
            return ctx.enter_context(nc.sbuf_tensor(name, shape, dt))

        def sem(name):
            return ctx.enter_context(nc.semaphore(name))

        ring = sb("ring", [P, NS, 4096])
        H = sb("H", [P, TB, D])
        XN = sb("XN", [P, TB, D])
        XT = sb("XT", [P, KC, S])
        WK1 = sb("WK1", [P, 2048])
        WK2 = sb("WK2", [P, 2048])
        WK3 = sb("WK3", [P, 2048])
        WK4 = sb("WK4", [P, 2048])
        ident = sb("ident", [P, P])
        before = sb("before", [P, P])
        ones = sb("ones", [P, P])
        chunk_mask = sb("chunk_mask", [P, P], I32)
        slot_iota = sb("slot_iota", [P, CAP])
        gains = sb("gains", [P, NG])
        lbt = sb("lbt", [P, 5, HEADS])
        rw = sb("rw", [P, 2, KC, LG])
        rb = sb("rb", [P, 2, LG])
        lam = sb("lam", [P, 4, DH])
        lams = sb("lams", [P, 6])
        sub_gain = sb("sub_gain", [P, 1])
        ssum = sb("ssum", [P, TB])
        rstd = sb("rstd", [P, TB])
        neg_half = sb("neg_half", [P, 16])
        hsum = sb("hsum", [P, 16])
        hrstd = sb("hrstd", [P, 16])
        chunk_decay = sb("chunk_decay", [P, HEADS, NCH])
        busiest = sb("busiest", [P, 2])
        busiest_i = sb("busiest_i", [P, 1], I32)
        lbt_last = sb("lbt_last", [P, 2, 32])
        att_s = sb("att_s", [P, 2, 16])

        chunk_mask_f = WK4[:, 0:P]
        gain_rows = WK4[0:NG, P:2 * P]
        QD = WK1[:, :].rearrange("p (h t) -> p h t", h=HEADS)
        KI = WK2[:, :].rearrange("p (h t) -> p h t", h=HEADS)
        KTOK = WK3[:, :].rearrange("p (b f) -> p b f", b=TB)
        GATE = WK4[:, :].rearrange("p (b f) -> p b f", b=TB)
        BC = ring[:, 7, 0:2048]
        KF = ring[:, 7, 2048:4096]
        EX = ring[:, 8, 0:2048]
        ST = ring[:, 8, 2048:4096].rearrange("p (b f) -> p b f", b=2)
        XT2 = WK2[:, :].rearrange("p (k t) -> p k t", k=KC)
        QT = WK1[:, :].rearrange("p (h t) -> p h t", h=HEADS)
        KT = WK3[:, :].rearrange("p (h t) -> p h t", h=HEADS)
        OB = WK4[:, :].rearrange("p (b f) -> p b f", b=TB)
        causal_neg = ring[:, 5, 0:384]
        SM = ring[:, 5, 512:512 + 1536].rearrange("p (b m c) -> p b m c", b=2, m=2)
        lamt = ring[:, 5, 3072:3072 + 2 * DH].rearrange("p (a d) -> p a d", a=2)
        PT = ring[:, 5, 2048:2048 + 768].rearrange("p (b c) -> p b c", b=2)
        XE = [WK1[:, 0:KC * GRP * CAP].rearrange("p (k c) -> p k c", k=KC),
              WK2[:, 0:KC * GRP * CAP].rearrange("p (k c) -> p k c", k=KC)]
        GD = WK3[:, 0:2 * TB * GRP * P].rearrange("p (b t e c) -> p b t e c", b=2, t=TB, e=GRP)
        PD = WK4[:, 0:2 * TB * GRP * CAP].rearrange("p (b t e c) -> p b t e c", b=2, t=TB, e=GRP)
        HS = WK4[:, 768:1024]
        HH = WK4[:, 1024:1280]
        HG = WK4[:, 1280:1792]
        logit = WK3[:, 1536:1608].rearrange("p (t n) -> p t n", t=TB)
        member = WK3[:, 1608:1672].rearrange("p (t n) -> p t n", t=TB)
        rt4 = WK3[:, 1672:1736].rearrange("p (t g j) -> p t g j", t=TB, g=G4)
        rt = WK3[:, 1736:1992].rearrange("p (i t w) -> p i t w", i=16, t=TB)
        gate = WK1[:, 1536:1536 + TB * SW].rearrange("p (t n) -> p t n", t=TB)
        slot = WK2[:, 1536:1536 + TB * SW].rearrange("p (t n) -> p t n", t=TB)
        YS = XT[:, 0:2, :].rearrange("p a b -> p (a b)")
        GROW = WK3[:, 0:D]
        OUTB = ring[:, 0, 0:2048].rearrange("p (b f) -> p b f", b=TB)

        PS = ctx.enter_context(nc.psum_tensor("PS", [P, 8, 512], F32))
        B_GU, B_XG, B_Y, B_TR = 4, 5, 6, 7

        landed = [sem(f"landed{i}") for i in range(NS)]
        x_landed = sem("x_landed")
        small_landed = sem("small_landed")
        lam_landed = sem("lam_landed")
        final_gain_landed = sem("final_gain_landed")
        out_written = sem("out_written")
        consts_ready = sem("consts_ready")
        gains_psum = sem("gains_psum")
        gains_ready = sem("gains_ready")
        lb_max = sem("lb_max")
        lb_exp = sem("lb_exp")
        act_own, dve_own, pool_own = sem("act_own"), sem("dve_own"), sem("pool_own")
        squares = sem("squares")
        variances = sem("variances")
        rstd_ready = sem("rstd_ready")
        xn0_ready, xn1_ready = sem("xn0_ready"), sem("xn1_ready")
        xt_psum = sem("xt_psum")
        xt_dve, xt_act = sem("xt_dve"), sem("xt_act")
        qf_psum, qf_sig, qf_free = sem("qf_psum"), sem("qf_sig"), sem("qf_free")
        qf_lin = sem("qf_lin")
        logf_ready, cum_ready = sem("logf_ready"), sem("cum_ready")
        exps_ready, rest_ready, rest_exp = sem("exps_ready"), sem("rest_ready"), sem("rest_exp")
        kend_ready = sem("kend_ready")
        v_psum, v_ready, g_psum, g_sig, gate_ready = (sem(n) for n in ("v_psum", "v_ready", "g_psum", "g_sig", "gate_ready"))
        kt_psum, ktok_ready = sem("kt_psum"), sem("ktok_ready")
        masked_zero, score_psum, score_ready = sem("masked_zero"), sem("score_psum"), sem("score_ready")
        kv_psum, state_ready, o_psum = sem("kv_psum"), sem("state_ready"), sem("o_psum")
        o_sq, o_var, o_rstd, o_ready = sem("o_sq"), sem("o_var"), sem("o_rstd"), sem("o_ready")
        ot_psum, ot_ready = sem("ot_psum"), sem("ot_ready")
        mix_psum, mixed = sem("mix_psum"), sem("mixed")
        kproj_psum, kproj_ready = sem("kproj_psum"), sem("kproj_ready")
        qproj_psum, qproj_ready = sem("qproj_psum"), sem("qproj_ready")
        vb_psum, vb_ready = sem("vb_psum"), sem("vb_ready")
        lam_dot, lam_exp = sem("lam_dot"), sem("lam_exp")
        causal_ready = sem("causal_ready")
        s_psum, s_max, s_exp, p_ready = sem("s_psum"), sem("s_max"), sem("s_exp"), sem("p_ready")
        pt_psum, pt_ready, ob_psum, ob_ready = sem("pt_psum"), sem("pt_ready"), sem("ob_psum"), sem("ob_ready")
        logits_psum = sem("logits_psum")
        coarse_in, coarse_exp, fine_in, fine_exp = sem("coarse_in"), sem("coarse_exp"), sem("fine_in"), sem("fine_exp")
        member_ready, ranks_psum, slots_ready = sem("member_ready"), sem("ranks_psum"), sem("slots_ready")

        class ExpertSems:
            def __init__(self, name):
                def s(n):
                    return sem(f"{name}_{n}")
                self.dispatch_built = s("dispatch_built")
                self.gates_built = s("gates_built")
                self.gathered = s("gathered")
                self.even_taken = s("even_taken")
                self.odd_taken = s("odd_taken")
                self.up_half = s("up_half")
                self.up_done = s("up_done")
                self.silu_done = s("silu_done")
                self.act_done = s("act_done")
                self.turned = s("turned")
                self.turned_taken = s("turned_taken")
                self.down_done = s("down_done")
                self.y_taken = s("y_taken")
                self.combined = s("combined")

        main_s = [ExpertSems(f"main{l}") for l in range(2)]
        more_s = [ExpertSems(f"more{l}") for l in range(2)]
        more_landed = [[sem(f"more{l}_landed{i}") for i in range(3)] for l in range(2)]
        more_shift = [sem(f"more{l}_shift") for l in range(2)]
        acc_done = sem("acc_done")
        moe_dve, moe_act = sem("moe_dve"), sem("moe_act")
        final_dve, final_act = sem("final_dve"), sem("final_act")

        used = [0] * NS

        def place(slot):
            used[slot] += 1
            return slot, 16 * used[slot]

        w_in = a_w_in[0].rearrange("(k p) n -> p k n", p=P)
        w_out_a = a_w_out[0].rearrange("(k p) n -> p k n", p=P)
        w_kvv = w_kv.rearrange("(k p) n -> p k n", p=P)
        w_qv = b_w_q[0].rearrange("(k p) n -> p k n", p=P)
        w_out_b = b_w_out[0].rearrange("(k p) n -> p k n", p=P)
        gu_v = [expert_w_gu[l].rearrange("e (k p) n -> p e k n", p=P) for l in range(2)]
        dn_v = [expert_w_down[l].rearrange("e (c p) n -> p e c n", p=P) for l in range(2)]

        def cols(s):
            return ring[:, s, :].rearrange("p (k n) -> p k n", k=KC)

        def rows(s):
            return ring[:, s, :].rearrange("p (k n) -> p k n", k=4)

        A_UNITS = {}
        for name, s in (("q0", 0), ("f0", 1), ("q1", 2), ("f1", 3), ("v0", 4), ("v1", 5), ("g0", 6),
                        ("g1", 4), ("o0", 5), ("o1", 6)):
            A_UNITS[name] = place(s)
        BASE = [None, None]
        ROT = [0, 5]
        BASE[0] = list(used)
        for u in range(3 * NE):
            used[(u + ROT[0]) % NS] += 1
        B_UNITS = {}
        for name, s in (("k0", 6), ("k1", 7), ("v0", 8), ("v1", 0), ("q0", 1), ("q1", 2), ("o0", 3), ("o1", 4)):
            B_UNITS[name] = place(s)
        BASE[1] = list(used)

        def unit_slot(layer, e, i):
            return (3 * (e % 3) + i + ROT[layer]) % NS

        def unit_count(layer, e, i, third):
            return (third + BASE[layer][unit_slot(layer, e, i)] + 1) * 16

        block = ctx.enter_context(nc.Block())

        @block.sync
        def _(sp):
            for b in range(TB):
                sp.dma_start(H[:, b, :], x[0, b * P:(b + 1) * P, :]).then_inc(x_landed, 16)
            for dst, n, src in ((GA_A, 8, a_norm_g[0]), (GA_LB, 8, a_lb[0]), (GA_LB + 8, 8, a_lb[1]),
                                (GA_KV, 8, kv_norm_g), (GA_B, 8, b_norm_g[0]), (GA_F, 8, ffn_norm_g[0]),
                                (GA_F + 8, 8, ffn_norm_g[1]), (GA_ON, 1, a_onorm_g[0]), (GA_SL, 1, b_subln_g[0])):
                sp.dma_start(gain_rows[dst:dst + n, :], src.rearrange("(k p) -> k p", p=P)).then_inc(small_landed, 16)

            def unit(table, name, dst, src):
                s, _ = table[name]
                sp.dma_start(dst(s), src).then_inc(landed[s], 16)

            for name, c in (("q0", 0), ("f0", 2), ("q1", 1), ("f1", 3), ("v0", 4), ("v1", 5), ("g0", 6)):
                unit(A_UNITS, name, cols, w_in[:, :, c * 512:(c + 1) * 512])
            for l in range(2):
                sp.dma_start(rw[:, l, :, 0:G4], router_g_w[l].rearrange("(k p) n -> p k n", p=P)).then_inc(lam_landed, 16)
                sp.dma_start(rw[:, l, :, G4:LG], router_e_w[l].rearrange("(k p) n -> p k n", p=P)).then_inc(lam_landed, 16)
                sp.dma_start(rb[:, l, 0:G4], router_g_b[l].partition_broadcast(P)).then_inc(lam_landed, 16)
                sp.dma_start(rb[:, l, G4:LG], router_e_b[l].partition_broadcast(P)).then_inc(lam_landed, 16)
            sp.dma_start(lam[:], b_lam[0].partition_broadcast(P)).then_inc(lam_landed, 16)
            sp.wait_ge(v_psum, 2)
            unit(A_UNITS, "g1", cols, w_in[:, :, 7 * 512:8 * 512])
            sp.wait_ge(v_psum, 4)
            unit(A_UNITS, "o0", rows, w_out_a[:, 0:4, :])
            sp.wait_ge(g_psum, 2)
            unit(A_UNITS, "o1", rows, w_out_a[:, 4:8, :])

            def expert_unit(l, e, j, i):
                s = unit_slot(l, j, i)
                if i < 2:
                    src = gu_v[l][:, bass.ds(e, 1), 4 * i:4 * i + 4, :]
                else:
                    src = dn_v[l][:, bass.ds(e, 1), :, :]
                sp.dma_start(ring[:, s, :].rearrange("p (e k n) -> p e k n", e=1, k=4), src).then_inc(landed[s], 16)

            def expert_layer(l, first_waits):
                es, xs = main_s[l], more_s[l]
                for u in range(9):
                    for s_, v_ in first_waits.get(u, ()):
                        sp.wait_ge(s_, v_)
                    expert_unit(l, u // 3, u // 3, u % 3)
                freed = (es.up_half, es.up_done, es.down_done)
                with sp.Fori(0, NE // 3 - 1) as g:
                    for j in range(3):
                        for i in range(3):
                            sp.wait_ge(freed[i], g * 3 + (j + 1))
                            expert_unit(l, g * 3 + (3 + j), j, i)
                for e in range(NE - NE % 3, NE):
                    for i in range(3):
                        sp.wait_ge(freed[i], e - 2)
                        expert_unit(l, e, e % 3, i)
                sp.wait_ge(slots_ready, l + 1)
                most = sp.value_load(busiest_i[0:1, 0:1], min_val=0, max_val=S)
                with sp.If(most > CAP):
                    sp.wait_ge(es.combined, NE)
                    with sp.Fori(0, (ROUNDS - 1)) as r:
                        with sp.Fori(0, NE) as e:
                            for i in range(3):
                                sp.wait_ge(xs.combined, r * NE + e + 1)
                                src = gu_v[l][:, bass.ds(e, 1), 4 * i:4 * i + 4, :] if i < 2 else dn_v[l][:, bass.ds(e, 1), :, :]
                                sp.dma_start(ring[:, i, :].rearrange("p (e k n) -> p e k n", e=1, k=4),
                                             src).then_inc(more_landed[l][i], 16)
                    sp.wait_ge(xs.combined, (ROUNDS - 1) * NE + 1)

            expert_layer(0, {0: [(qf_psum, 4)], 2: [(qf_psum, 8)], 4: [(g_psum, 4)], 5: [(mix_psum, 4)],
                             7: [(ot_psum, 4), (ot_ready, 4)]})
            es = main_s[0]
            last = {6: (es.up_half, 30), 7: (es.up_done, 30), 8: (es.down_done, 30), 0: (es.up_half, 31),
                    1: (es.up_done, 31), 2: (es.down_done, 31), 3: (es.up_half, 32), 4: (es.up_done, 32)}
            for name, dst, src in (("k0", cols, w_kvv[:, :, 0:512]), ("k1", cols, w_kvv[:, :, 512:1024]),
                                   ("v0", cols, w_kvv[:, :, 1024:1536]), ("v1", cols, w_kvv[:, :, 1536:2048]),
                                   ("q0", cols, w_qv[:, :, 0:512]), ("q1", cols, w_qv[:, :, 512:1024]),
                                   ("o0", rows, w_out_b[:, 0:4, :]), ("o1", rows, w_out_b[:, 4:8, :])):
                sp.wait_ge(*last[B_UNITS[name][0]])
                unit(B_UNITS, name, dst, src)
            expert_layer(1, {0: [(ot_psum, 8), (ot_ready, 8)], 1: [(kproj_psum, 4)], 3: [(vb_psum, 2)], 4: [(vb_psum, 4)],
                             5: [(qproj_psum, 4)], 7: [(mix_psum, 8)]})
            sp.wait_ge(acc_done, 2)
            sp.dma_start(GROW, final_norm_g.partition_broadcast(P)).then_inc(final_gain_landed, 16)
            sp.wait_ge(final_dve, 1)
            sp.dma_start(out[0, 0:P, :], OUTB[:, 0, :]).then_inc(out_written, 16)
            sp.wait_ge(final_act, 1)
            sp.dma_start(out[0, P:S, :], OUTB[:, 1, :]).then_inc(out_written, 16)
            sp.wait_ge(out_written, 32)

        @block.gpsimd
        def _(pool):
            own = Chain(pool, pool_own)
            gp = nc.gpsimd
            own.link(gp.memset(ident[:], 0.0))
            gp.affine_select(out=ident[:], in_=ident[:], compare_op=ALU.not_equal, fill=1.0, base=0,
                             pattern=[[-1, P]], channel_multiplier=1).then_inc(consts_ready, 1)
            gp.memset(neg_half[:], -0.5).then_inc(consts_ready, 1)
            gp.memset(ones[:], 1.0).then_inc(consts_ready, 1)
            pool.wait_ge(consts_ready, 3)
            gp.affine_select(out=before[:], in_=ones[:], compare_op=ALU.is_ge, fill=0.0, base=-1,
                             pattern=[[1, P]], channel_multiplier=-1).then_inc(consts_ready, 1)
            gp.iota(slot_iota[:], [[1, CAP]], base=0, channel_multiplier=0,
                    allow_small_or_imprecise_dtypes=True).then_inc(consts_ready, 1)
            own.link(gp.affine_select(out=chunk_mask_f, in_=ones[:], compare_op=ALU.is_ge, fill=0.0, base=0,
                                      pattern=[[1, P]], channel_multiplier=-1))
            cm = chunk_mask_f.rearrange("p (b c) -> p b c", c=CH)
            own.link(gp.affine_select(out=cm, in_=cm, compare_op=ALU.is_ge, fill=0.0, base=0,
                                      pattern=[[-CH, P // CH], [0, CH]], channel_multiplier=1))
            gp.tensor_copy(chunk_mask[:], chunk_mask_f).then_inc(consts_ready, 1)

            def norm(i):
                pool.wait_ge(variances, i + 1)
                gp.tensor_tensor(rstd[:], ssum[:], neg_half[:, 0:TB], ALU.pow).then_inc(rstd_ready, 1)

            def head_norm(i):
                pool.wait_ge(o_var, i + 1)
                gp.tensor_tensor(hrstd[:], hsum[:], neg_half[:], ALU.pow).then_inc(o_rstd, 1)

            def build_gates(es, buf, e, n, count):
                pool.wait_ge(es.dispatch_built, count)
                for t in range(TB):
                    for dup in range(2):
                        gp.tensor_tensor(GD[:, buf, t, 0:n, dup * CAP:(dup + 1) * CAP], PD[:, buf, t, 0:n, :],
                                         gate[:, t, bass.ds(e, n)].unsqueeze(2).to_broadcast([P, n, CAP]),
                                         ALU.mult).then_inc(es.gates_built, 1)

            def expert_layer(l):
                es, xs = main_s[l], more_s[l]
                pool.wait_ge(slots_ready, l + 1)
                build_gates(es, 0, 0, GRP, 1)
                build_gates(es, 1, GRP, GRP, 2)
                with pool.Fori(0, 4) as it:
                    for b in range(2):
                        pool.wait_ge(es.turned, it * 6 + (3 * b + 3))
                        build_gates(es, b, it * 6 + (6 + 3 * b), GRP, it * 2 + (b + 3))
                pool.wait_ge(es.turned, 27)
                build_gates(es, 0, 30, GRP, 11)
                most = pool.value_load(busiest_i[0:1, 0:1], min_val=0, max_val=S)
                with pool.If(most > CAP):
                    with pool.Fori(0, ROUNDS - 1) as r:
                        with pool.Fori(0, NE) as e:
                            build_gates(xs, 0, e, 1, r * NE + e + 1)

            norm(0)
            pool.wait_ge(kend_ready, 2)
            gp.memset(EX, 0.0).then_inc(masked_zero, 1)
            head_norm(0)
            norm(1)
            expert_layer(0)
            norm(2)
            pool.wait_ge(moe_dve, 1)
            own.link(gp.memset(causal_neg, 0.0))
            for c0 in (0, 256):
                gp.affine_select(out=causal_neg[:, c0:c0 + P], in_=causal_neg[:, c0:c0 + P], compare_op=ALU.is_ge,
                                 fill=NEG, base=0, pattern=[[-1, P]], channel_multiplier=1).then_inc(causal_ready, 1)
            head_norm(1)
            norm(3)
            expert_layer(1)
            norm(4)

        @block.tensor
        def _(pe):
            mm, tr = nc.tensor.matmul, nc.tensor.transpose

            def norm(i):
                if i == 0:
                    pe.wait_ge(consts_ready, 1)
                pe.wait_ge(xn0_ready, i + 1)
                pe.wait_ge(xn1_ready, i + 1)
                for b in range(4):
                    for j in range(2):
                        k = 2 * b + j
                        for t in range(TB):
                            last = tr(PS[:, 4 + b, j * S + t * P:j * S + (t + 1) * P], XN[:, t, k * P:(k + 1) * P], ident[:])
                    last.then_inc(xt_psum, 1)

            def token_major(bank, src, t, w, sem_):
                for k in range(KC):
                    last = mm(PS[:, bank, :], src[:, k, t * P:(t + 1) * P], w(k), start=(k == 0), stop=(k == KC - 1))
                last.then_inc(sem_, 1)

            def mix_out(i, units):
                pe.wait_ge(ot_ready, 4 * (i + 1))
                for n in ("o0", "o1"):
                    pe.wait_ge(landed[units[n][0]], units[n][1])
                for t in range(TB):
                    for nh in range(2):
                        token_major(2 * t + nh, XT, t,
                                    lambda k: rows(units["o0" if k < 4 else "o1"][0])[:, k % 4, nh * 512:(nh + 1) * 512],
                                    mix_psum)

            def turn_heads(src, i):
                for b in range(4):
                    for j in range(2):
                        h = 2 * b + j
                        for t in range(TB):
                            last = tr(PS[:, 4 + b, j * S + t * P:j * S + (t + 1) * P], src[:, t, h * P:(h + 1) * P], ident[:])
                    last.then_inc(ot_psum, 1)

            pe.wait_ge(consts_ready, 1)
            pe.wait_ge(small_landed, 16 * 9)
            tr(PS[:, 0, 0:NG], gain_rows, ident[0:NG, 0:NG]).then_inc(gains_psum, 1)
            norm(0)
            pe.wait_ge(gains_ready, 1)
            pe.wait_ge(xt_dve, 4)
            pe.wait_ge(xt_act, 4)
            for h in range(HEADS):
                if h % 4 == 0:
                    for n in ("q", "f"):
                        pe.wait_ge(landed[A_UNITS[f"{n}{h // 4}"][0]], A_UNITS[f"{n}{h // 4}"][1])
                if h >= 4:
                    pe.wait_ge(qf_free, h - 3)
                for j, n in enumerate(("q", "f")):
                    w = cols(A_UNITS[f"{n}{h // 4}"][0])
                    c = (h % 4) * P
                    for k in range(KC):
                        last = mm(PS[:, h % 4, j * S:(j + 1) * S], w[:, k, c:c + P], XT[:, k, :],
                                  start=(k == 0), stop=(k == KC - 1))
                last.then_inc(qf_psum, 1)
            for nh in range(2):
                pe.wait_ge(landed[A_UNITS[f"v{nh}"][0]], A_UNITS[f"v{nh}"][1])
                for t in range(TB):
                    token_major(4 + 2 * nh + t, XT, t, lambda k: cols(A_UNITS[f"v{nh}"][0])[:, k, :], v_psum)
            pe.wait_ge(qf_free, HEADS)
            for nh in range(2):
                pe.wait_ge(landed[A_UNITS[f"g{nh}"][0]], A_UNITS[f"g{nh}"][1])
                for t in range(TB):
                    token_major(2 * nh + t, XT, t, lambda k: cols(A_UNITS[f"g{nh}"][0])[:, k, :], g_psum)
            pe.wait_ge(v_ready, 4)
            pe.wait_ge(kend_ready, 2)
            KFh = KF.rearrange("p (h t) -> p h t", h=HEADS)
            for t in range(TB):
                for hh in range(2):
                    for h in range(4 * hh, 4 * hh + 4):
                        last = tr(PS[:, 4 + 2 * t + hh, (h % 4) * P:(h % 4 + 1) * P], KFh[:, h, t * P:(t + 1) * P], ident[:])
                    last.then_inc(kt_psum, 1)
            pe.wait_ge(ktok_ready, 4)
            SC = EX.rearrange("p (h t) -> p h t", h=HEADS)
            VA = XN

            def intra(t, nh):
                for hh in range(4):
                    h = 4 * nh + hh
                    mm(PS[:, 2 * t + nh, hh * P:(hh + 1) * P], SC[:, h, t * P:(t + 1) * P], VA[:, t, h * P:(h + 1) * P],
                       start=(hh == 0), stop=True, skip_group_check=True)

            for h in range(HEADS):
                if h >= 4:
                    pe.wait_ge(score_ready, h - 3)
                for t in range(TB):
                    last = mm(PS[:, 4 + h % 4, t * P:(t + 1) * P], KI[:, h, t * P:(t + 1) * P], QD[:, h, t * P:(t + 1) * P],
                              start=True, stop=True)
                last.then_inc(score_psum, 1)
            pe.wait_ge(score_ready, HEADS)
            pe.wait_ge(gate_ready, 4)

            def chunk_kv(n):
                r, t = CH * (n % 4), n // 4
                for h in range(HEADS):
                    last = mm(PS[:, 4 + 2 * (n % 2) + h // 4, (h % 4) * P:(h % 4 + 1) * P],
                              KTOK[r:r + CH, t, h * P:(h + 1) * P], VA[r:r + CH, t, h * P:(h + 1) * P],
                              start=True, stop=True, tile_position=(r, 0))
                last.then_inc(kv_psum, 1)

            chunk_kv(0)
            chunk_kv(1)
            for t in range(TB):
                for nh in range(2):
                    intra(t, nh)
            for n in range(1, NCH):
                pe.wait_ge(state_ready, n)
                r, t = CH * (n % 4), n // 4
                if n + 1 < NCH - 1:
                    chunk_kv(n + 1)
                for h in range(HEADS):
                    last = mm(PS[r:r + CH, 2 * t + h // 4, (h % 4) * P:(h % 4 + 1) * P],
                              QD[:, h, n * CH:(n + 1) * CH], ST[:, n % 2, h * P:(h + 1) * P],
                              start=False, stop=True, skip_group_check=True, tile_position=(0, r))
                last.then_inc(o_psum, 1)
            pe.wait_ge(o_ready, 1)
            turn_heads(BC.rearrange("p (b f) -> p b f", b=TB), 0)
            mix_out(0, A_UNITS)

            def gather_fill(es, xn_k, pd, q, width, bank):
                for j in range(2):
                    k = 2 * q + j
                    for t in range(TB):
                        last = mm(PS[:, bank, j * width:(j + 1) * width], XN[:, t, k * P:(k + 1) * P], pd[:, t],
                                  start=(t == 0), stop=(t == TB - 1))
                last.then_inc(es.gathered, 1)

            def gather(es, buf, group):
                pe.wait_ge(es.dispatch_built, group + 1)
                pd = PD[:, buf, :, :, :].rearrange("p t e c -> p t (e c)")
                gather_fill(es, XN, pd, 0, GRP * CAP, B_XG)
                gather_fill(es, XN, pd, 1, GRP * CAP, B_Y)
                pe.wait_ge(es.even_taken, group * 2 + 1)
                gather_fill(es, XN, pd, 2, GRP * CAP, B_XG)
                pe.wait_ge(es.odd_taken, group * 2 + 1)
                gather_fill(es, XN, pd, 3, GRP * CAP, B_Y)

            def up(es, xe, wa, wb, wait_a, wait_b):
                for i, (w, wait) in enumerate(((wa, wait_a), (wb, wait_b))):
                    pe.wait_ge(*wait)
                    for kk in range(4):
                        k = 4 * i + kk
                        cw = w[:, kk, :].rearrange("p (a h f) -> p a h f", a=2, h=2)
                        for half in range(2):
                            last = mm(PS[CAP * half:CAP * (half + 1), B_GU, :].rearrange("p (a f) -> p a f", a=2), xe(k),
                                      cw[:, :, half, :], start=(k == 0), stop=(k == KC - 1), tile_position=(0, CAP * half))
                    last.then_inc(es.up_half if i == 0 else es.up_done, 1)

            def turn(es, gd, count, gates_count):
                pe.wait_ge(es.gates_built, gates_count)
                pe.wait_ge(es.act_done, count)
                for j in range(2):
                    tr(PS[:, B_TR, j * P:(j + 1) * P], HH[:, j * P:(j + 1) * P], ident[:])
                for t in range(TB):
                    last = tr(PS[:, B_TR, (2 + t) * P:(3 + t) * P], gd[:, t], ident[:])
                last.then_inc(es.turned, 1)

            def down(es, w, wait, count):
                pe.wait_ge(*wait)
                pe.wait_ge(es.turned_taken, count)
                for c in range(4):
                    half, j = c // 2, c % 2
                    for nh in range(2):
                        last = mm(PS[CAP * nh:CAP * (nh + 1), B_Y, :], HG[:, j * P + half * CAP:j * P + (half + 1) * CAP],
                                  w[:, c, nh * 512:(nh + 1) * 512], start=(c == 0), stop=(c == 3),
                                  tile_position=(0, CAP * nh))
                last.then_inc(es.down_done, 1)

            def combine(es, count):
                pe.wait_ge(es.y_taken, count)
                for t in range(TB):
                    for nh in range(2):
                        last = mm(PS[:, 2 * t + nh, :], HG[CAP * nh:CAP * (nh + 1), (2 + t) * P:(3 + t) * P],
                                  YS[CAP * nh:CAP * (nh + 1), :], start=False, stop=True, skip_group_check=True,
                                  tile_position=(CAP * nh, 0))
                last.then_inc(es.combined, 1)

            def expert_layer(l):
                es, xs = main_s[l], more_s[l]
                pe.wait_ge(xt_dve, 4 * l + 8 + 4 * l)
                pe.wait_ge(xt_act, 4 * l + 8 + 4 * l)
                if l == 0:
                    pe.wait_ge(lam_landed, 16 * 9)
                for t in range(TB):
                    for k in range(KC):
                        last = mm(PS[:, B_XG, t * LG:(t + 1) * LG], XT[:, k, t * P:(t + 1) * P], rw[:, l, k, :],
                                  start=(k == 0), stop=(k == KC - 1))
                last.then_inc(logits_psum, 1)
                for t in range(TB):
                    for nh in range(2):
                        mm(PS[:, 2 * t + nh, :], ident[:], H[:, t, nh * 512:(nh + 1) * 512], start=True, stop=True)
                pe.wait_ge(member_ready, l + 1)
                if l == 0:
                    pe.wait_ge(consts_ready, 5)
                mm(PS[:, B_XG, 0:NE], before[:], member[:, 0, :], start=True, stop=True)
                mm(PS[:, B_XG, NE:2 * NE], ones[:], member[:, 0, :], start=True, stop=False)
                mm(PS[:, B_XG, NE:2 * NE], before[:], member[:, 1, :], start=False, stop=True)
                mm(PS[:, B_XG, 2 * NE:3 * NE], ones[:], member[:, 0, :], start=True, stop=False)
                mm(PS[:, B_XG, 2 * NE:3 * NE], ones[:], member[:, 1, :], start=False, stop=True).then_inc(ranks_psum, 1)
                pe.wait_ge(slots_ready, l + 1)
                gather(es, 0, 0)

                def step(j6, e, third, group, with_next, defer):
                    buf, jj = (j6 // 3) % 2, j6 % 3
                    if jj == 0:
                        pe.wait_ge(es.even_taken, group * 2 + 2)
                        pe.wait_ge(es.odd_taken, group * 2 + 2)
                    units = [unit_slot(l, j6, i) for i in range(3)]
                    waits = [(landed[units[i]], unit_count(l, j6, i, third)) for i in range(3)]
                    up(es, lambda k: XE[buf][:, k, jj * CAP:(jj + 1) * CAP], rows(units[0]), rows(units[1]), waits[0], waits[1])
                    if jj > 0:
                        combine(es, e)
                    elif with_next:
                        gather(es, 1 - buf, group + 1)
                    turn(es, GD[:, buf, :, jj, :], e + 1, (group + 1) * 4)
                    if jj == 0 and with_next:
                        pe.wait_ge(es.odd_taken, group * 2 + 4)
                    down(es, rows(units[2]), waits[2], e + 1)
                    if jj == 2 or not defer:
                        combine(es, e + 1)

                with pe.Fori(0, 5) as it:
                    for j6 in range(6):
                        step(j6, it * 6 + j6, it * 2 + j6 // 3, it * 2 + j6 // 3, True, True)
                step(0, 30, 10, 10, False, True)
                step(1, 31, 10, 10, False, False)

                most = pe.value_load(busiest_i[0:1, 0:1], min_val=0, max_val=S)
                with pe.If(most > CAP):
                    pe.wait_ge(es.combined, NE)
                    pe.sem_inc(xs.combined, 1)
                    with pe.Fori(0, ROUNDS - 1) as r:
                        with pe.Fori(0, NE) as e:
                            n = r * NE + e
                            pe.wait_ge(xs.dispatch_built, n + 1)
                            for k in range(KC):
                                for t in range(TB):
                                    last = mm(PS[:, B_XG, k * CAP:(k + 1) * CAP], XN[:, t, k * P:(k + 1) * P],
                                              PD[:, 0, t, 0, :], start=(t == 0), stop=(t == TB - 1))
                            last.then_inc(xs.gathered, 1)
                            pe.wait_ge(xs.even_taken, n + 1)
                            up(xs, lambda k: XE[0][:, k, 0:CAP], rows(0), rows(1),
                               (more_landed[l][0], n * 16 + 16), (more_landed[l][1], n * 16 + 16))
                            turn(xs, GD[:, 0, :, 0, :], n + 1, (n + 1) * 4)
                            down(xs, rows(2), (more_landed[l][2], n * 16 + 16), n + 1)
                            combine(xs, n + 1)
                    pe.wait_ge(xs.combined, (ROUNDS - 1) * NE + 1)
                pe.wait_ge(es.combined, NE)
                pe.sem_inc(acc_done, 1)

            norm(1)
            expert_layer(0)

            norm(2)
            pe.wait_ge(moe_dve, 1)
            pe.wait_ge(moe_act, 1)
            pe.wait_ge(xt_dve, 12)
            pe.wait_ge(xt_act, 12)
            for h in range(HEADS):
                if h % 4 == 0:
                    pe.wait_ge(landed[B_UNITS[f"k{h // 4}"][0]], B_UNITS[f"k{h // 4}"][1])
                w = cols(B_UNITS[f"k{h // 4}"][0])
                for k in range(KC):
                    last = mm(PS[:, h // 2, (h % 2) * S:(h % 2 + 1) * S], w[:, k, (h % 4) * P:(h % 4 + 1) * P], XT[:, k, :],
                              start=(k == 0), stop=(k == KC - 1))
                if h % 2:
                    last.then_inc(kproj_psum, 1)
            for nh in range(2):
                pe.wait_ge(landed[B_UNITS[f"v{nh}"][0]], B_UNITS[f"v{nh}"][1])
                for t in range(TB):
                    token_major(4 + 2 * nh + t, XT, t, lambda k: cols(B_UNITS[f"v{nh}"][0])[:, k, :], vb_psum)
            pe.wait_ge(kproj_ready, 4)
            for h in range(HEADS):
                if h % 4 == 0:
                    pe.wait_ge(landed[B_UNITS[f"q{h // 4}"][0]], B_UNITS[f"q{h // 4}"][1])
                w = cols(B_UNITS[f"q{h // 4}"][0])
                for k in range(KC):
                    last = mm(PS[:, h // 2, (h % 2) * S:(h % 2 + 1) * S], w[:, k, (h % 4) * P:(h % 4 + 1) * P], XT2[:, k, :],
                              start=(k == 0), stop=(k == KC - 1))
                if h % 2:
                    last.then_inc(qproj_psum, 1)
            pe.wait_ge(vb_ready, 4)
            pe.wait_ge(qproj_ready, 4)

            def scores(h):
                if h >= 2:
                    pe.wait_ge(s_max, 2 * (h - 1))
                for m in range(2):
                    r, bank = DH * m, 4 + 2 * (h % 2) + m
                    mm(PS[:, bank, 0:P], QT[r:r + DH, h, 0:P], KT[r:r + DH, h, 0:P], start=True, stop=True,
                       tile_position=(r, 0))
                    last = mm(PS[:, bank, P:3 * P], QT[r:r + DH, h, P:S], KT[r:r + DH, h, :], start=True, stop=True,
                              tile_position=(r, 0))
                last.then_inc(s_psum, 1)

            def values(h):
                pe.wait_ge(p_ready, h + 1)
                if h >= 2:
                    pe.wait_ge(pt_ready, h - 1)
                for j in range(3):
                    last = tr(PS[:, h % 2, j * P:(j + 1) * P], SM[:, h % 2, 0, j * P:(j + 1) * P], ident[:])
                last.then_inc(pt_psum, 1)
                pe.wait_ge(pt_ready, h + 1)
                if h >= 2:
                    pe.wait_ge(ob_ready, h - 1)
                v = XN[:, :, h * P:(h + 1) * P]
                mm(PS[:, 2 + h % 2, 0:P], PT[:, h % 2, 0:P], v[:, 0, :], start=True, stop=True)
                mm(PS[:, 2 + h % 2, P:S], PT[:, h % 2, P:2 * P], v[:, 0, :], start=True, stop=False)
                mm(PS[:, 2 + h % 2, P:S], PT[:, h % 2, 2 * P:3 * P], v[:, 1, :], start=False, stop=True).then_inc(ob_psum, 1)

            scores(0)
            for h in range(1, HEADS):
                scores(h)
                values(h - 1)
            values(HEADS - 1)
            pe.wait_ge(o_ready, 2)
            turn_heads(OB, 1)
            pe.wait_ge(ob_ready, HEADS)
            mix_out(1, B_UNITS)
            norm(3)
            expert_layer(1)

        @block.scalar
        def _(act):
            own = Chain(act, act_own)
            af = nc.scalar.activation

            def norm(i, turn=True, second=None):
                for t in range(TB):
                    af(XN[:, t, :], H[:, t, :], ACT.Square, accum_out=ssum[:, t:t + 1]).then_inc(squares, 1)
                act.wait_ge(rstd_ready, i + 1)
                dst = XN[:, 1, :] if turn else OUTB[:, 1, :]
                af(dst, H[:, 1, :], ACT.Identity, scale=rstd[:, 1:2]).then_inc(xn1_ready, 1)
                if not turn:
                    return
                if i == 0:
                    act.wait_ge(gains_ready, 1)
                for b in (2, 3):
                    act.wait_ge(xt_psum, 4 * i + b + 1)
                    for j in range(2):
                        k = 2 * b + j
                        g = {0: GA_A, 1: GA_F, 2: GA_KV, 3: GA_F + 8}[i]
                        if i == 2:
                            own.link(af(XT2[:, k, :], PS[:, 4 + b, j * S:(j + 1) * S], ACT.Identity,
                                        scale=gains[:, GA_B + k:GA_B + k + 1]))
                        af(XT[:, k, :], PS[:, 4 + b, j * S:(j + 1) * S], ACT.Identity,
                           scale=gains[:, g + k:g + k + 1]).then_inc(xt_act, 1)

            act.wait_ge(x_landed, 32)
            norm(0)
            act.wait_ge(lb_max, 1)
            af(lbt[:, 0:2, :], lbt[:, 0:2, :], ACT.Exp).then_inc(lb_exp, 1)
            for h in range(HEADS):
                act.wait_ge(qf_psum, h + 1)
                af(QD[:, h, :], PS[:, h % 4, 0:S], ACT.Sigmoid)
                af(BC[:, h * S:(h + 1) * S], PS[:, h % 4, S:2 * S], ACT.Sigmoid)
                af(KF[:, h * S:(h + 1) * S], PS[:, h % 4, S:2 * S], ACT.Sigmoid, scale=-1.0).then_inc(qf_sig, 1)
            for hf in range(2):
                act.wait_ge(qf_lin, 4 * (hf + 1))
                c = slice(hf * 1024, (hf + 1) * 1024)
                af(BC[:, c], BC[:, c], ACT.Ln).then_inc(logf_ready, 1)
            for hf in range(2):
                act.wait_ge(cum_ready, hf + 1)
                c = slice(hf * 1024, (hf + 1) * 1024)
                af(EX[:, c], BC[:, c], ACT.Exp)
                af(WK2[:, c], BC[:, c], ACT.Exp, scale=-1.0).then_inc(exps_ready, 1)
            for hf in range(2):
                act.wait_ge(rest_ready, hf + 1)
                c = slice(hf * 1024, (hf + 1) * 1024)
                af(EX[:, c], BC[:, c], ACT.Exp).then_inc(rest_exp, 1)
            for nh in range(2):
                for t in range(TB):
                    act.wait_ge(v_psum, 2 * nh + t + 1)
                    nc.scalar.copy(XN[:, t, nh * 512:(nh + 1) * 512], PS[:, 4 + 2 * nh + t, :]).then_inc(v_ready, 1)
            for nh in range(2):
                for t in range(TB):
                    act.wait_ge(g_psum, 2 * nh + t + 1)
                    af(GATE[:, t, nh * 512:(nh + 1) * 512], PS[:, 2 * nh + t, :], ACT.Sigmoid).then_inc(g_sig, 1)
            for t in range(TB):
                for hh in range(2):
                    act.wait_ge(kt_psum, 2 * t + hh + 1)
                    nc.scalar.copy(KTOK[:, t, hh * 512:(hh + 1) * 512], PS[:, 4 + 2 * t + hh, :]).then_inc(ktok_ready, 1)
            act.wait_ge(o_psum, NCH - 1)
            for b in range(4):
                af(BC[:, b * 512:(b + 1) * 512], PS[:, b, :], ACT.Square).then_inc(o_sq, 1)

            def turned_heads(i, gain, banks):
                for b in banks:
                    act.wait_ge(ot_psum, 4 * i + b + 1)
                    af(XT[:, 2 * b:2 * b + 2, :], PS[:, 4 + b, :].rearrange("p (a t) -> p a t", a=2), ACT.Identity,
                       scale=gain).then_inc(ot_ready, 1)

            turned_heads(0, gains[:, GA_ON:GA_ON + 1], range(4))

            def expert_layer(l):
                es, xs = main_s[l], more_s[l]
                act.wait_ge(coarse_in, l + 1)
                af(rt[:, 1, :, 0:G4], rt[:, 0, :, 0:G4], ACT.Exp).then_inc(coarse_exp, 1)
                act.wait_ge(fine_in, l + 1)
                af(rt[:, 9, :, 0:1], rt[:, 8, :, 0:1], ACT.Exp).then_inc(fine_exp, 1)

                def odd_fills(buf, group):
                    for q in (1, 3):
                        act.wait_ge(es.gathered, group * 4 + (q + 1))
                        for j in range(2):
                            k = 2 * q + j
                            last = af(XE[buf][:, k, :], PS[:, B_Y, j * GRP * CAP:(j + 1) * GRP * CAP], ACT.Identity,
                                      scale=gains[:, GA_F + 8 * l + k:GA_F + 8 * l + k + 1])
                        last.then_inc(es.odd_taken, 1)

                def silu(es_, count):
                    act.wait_ge(es_.up_done, count)
                    af(HS, PS[:, B_GU, 0:S], ACT.Silu).then_inc(es_.silu_done, 1)

                def take_y(es_, count):
                    act.wait_ge(es_.down_done, count)
                    nc.scalar.copy(YS, PS[:, B_Y, :]).then_inc(es_.y_taken, 1)

                odd_fills(0, 0)

                def step(j6, e, group, with_next):
                    silu(es, e + 1)
                    if j6 % 3 == 0 and with_next:
                        odd_fills(1 - (j6 // 3) % 2, group + 1)
                    take_y(es, e + 1)

                with act.Fori(0, 5) as it:
                    for j6 in range(6):
                        step(j6, it * 6 + j6, it * 2 + j6 // 3, True)
                step(0, 30, 10, False)
                step(1, 31, 10, False)
                most = act.value_load(busiest_i[0:1, 0:1], min_val=0, max_val=S)
                with act.If(most > CAP):
                    with act.Fori(0, ROUNDS - 1) as r:
                        with act.Fori(0, NE) as e:
                            silu(xs, r * NE + e + 1)
                            take_y(xs, r * NE + e + 1)
                act.wait_ge(acc_done, l + 1)
                for nh in range(2):
                    last = nc.scalar.copy(H[:, 1, nh * 512:(nh + 1) * 512], PS[:, 2 + nh, :])
                last.then_inc(moe_act, 1)
                act.wait_ge(moe_act, l + 1)
                act.wait_ge(moe_dve, l + 1)

            act.wait_ge(mixed, 4)
            norm(1)
            expert_layer(0)
            norm(2)
            act.wait_ge(lam_dot, 1)
            af(lams[:, 2:4], lams[:, 0:2], ACT.Exp).then_inc(lam_exp, 1)
            for b in range(4):
                act.wait_ge(kproj_psum, b + 1)
                nc.scalar.copy(KT[:, 2 * b:2 * b + 2, :], PS[:, b, :].rearrange("p (a t) -> p a t", a=2)).then_inc(kproj_ready, 1)
            for nh in range(2):
                for t in range(TB):
                    act.wait_ge(vb_psum, 2 * nh + t + 1)
                    nc.scalar.copy(XN[:, t, nh * 512:(nh + 1) * 512], PS[:, 4 + 2 * nh + t, :]).then_inc(vb_ready, 1)
            for b in range(4):
                act.wait_ge(qproj_psum, b + 1)
                nc.scalar.copy(QT[:, 2 * b:2 * b + 2, :], PS[:, b, :].rearrange("p (a t) -> p a t", a=2)).then_inc(qproj_ready, 1)

            def exps(h):
                act.wait_ge(s_max, 2 * (h + 1))
                a = att_s[:, h % 2, :]
                for m in range(2):
                    for b, c in ((0, slice(0, P)), (1, slice(P, 3 * P))):
                        i = 2 * m + b
                        v = SM[:, h % 2, m, c]
                        last = af(v, v, ACT.Exp, bias=a[:, 4 + i:5 + i], accum_out=a[:, 8 + i:9 + i])
                last.then_inc(s_exp, 1)

            def outputs(h):
                act.wait_ge(pt_psum, h + 1)
                nc.scalar.copy(PT[:, h % 2, :], PS[:, h % 2, 0:3 * P]).then_inc(pt_ready, 1)
                act.wait_ge(ob_psum, h + 1)
                for b in range(TB):
                    af(OB[:, b, h * P:(h + 1) * P], PS[:, 2 + h % 2, b * P:(b + 1) * P], ACT.Square,
                       accum_out=hsum[:, b * HEADS + h:b * HEADS + h + 1]).then_inc(act_own, 1)
                own.n += TB
                act.wait_ge(act_own, own.n)
                nc.scalar.copy(OB[:, :, h * P:(h + 1) * P],
                               PS[:, 2 + h % 2, 0:S].rearrange("p (b c) -> p b c", b=TB)).then_inc(ob_ready, 1)

            exps(0)
            for h in range(1, HEADS):
                exps(h)
                outputs(h - 1)
            outputs(HEADS - 1)
            turned_heads(1, sub_gain[:, 0:1], range(4))
            act.wait_ge(mixed, 8)
            norm(3)
            expert_layer(1)
            norm(4, turn=False)
            act.wait_ge(xn1_ready, 5)
            act.wait_ge(final_gain_landed, 16)

        @block.vector
        def _(dve):
            own = Chain(dve, dve_own)
            vt, vs, stt, red = nc.vector.tensor_tensor, nc.vector.tensor_scalar, nc.vector.scalar_tensor_tensor, nc.vector.tensor_reduce

            def norm(i, turn=True):
                dve.wait_ge(squares, 2 * (i + 1))
                vs(ssum[:], ssum[:], 1.0 / D, 1e-6, ALU.mult, ALU.add).then_inc(variances, 1)
                dve.wait_ge(rstd_ready, i + 1)
                dst = XN[:, 0, :] if turn else OUTB[:, 0, :]
                vs(dst, H[:, 0, :], rstd[:, 0:1], None, ALU.mult).then_inc(xn0_ready, 1)
                if not turn:
                    return
                for b in (0, 1):
                    dve.wait_ge(xt_psum, 4 * i + b + 1)
                    for j in range(2):
                        k = 2 * b + j
                        g = {0: GA_A, 1: GA_F, 2: GA_KV, 3: GA_F + 8}[i]
                        if i == 2:
                            own.link(vs(XT2[:, k, :], PS[:, 4 + b, j * S:(j + 1) * S], gains[:, GA_B + k:GA_B + k + 1], None, ALU.mult))
                        vs(XT[:, k, :], PS[:, 4 + b, j * S:(j + 1) * S], gains[:, g + k:g + k + 1], None,
                           ALU.mult).then_inc(xt_dve, 1)

            dve.wait_ge(gains_psum, 1)
            nc.vector.tensor_copy(gains[:], PS[:, 0, 0:NG]).then_inc(gains_ready, 1)
            dve.wait_ge(gains_ready, 1)
            l0, l1 = gains[:, GA_LB:GA_LB + 8], gains[:, GA_LB + 8:GA_LB + 16]
            own.link(vs(sub_gain[:], gains[:, GA_SL:GA_SL + 1], 1.0 - LAM_INIT, None, ALU.mult))
            own.link(vt(lbt[:, 2, :], l0, l1, ALU.max))
            own.link(vt(lbt[:, 0, :], l0, lbt[:, 2, :], ALU.subtract))
            vt(lbt[:, 1, :], l1, lbt[:, 2, :], ALU.subtract).then_inc(lb_max, 1)
            norm(0)
            dve.wait_ge(lb_exp, 1)
            own.link(vt(lbt[:, 2, :], lbt[:, 0, :], lbt[:, 1, :], ALU.add))
            own.link(nc.vector.reciprocal(lbt[:, 2, :], lbt[:, 2, :]))
            own.link(vt(lbt[:, 3, :], lbt[:, 0, :], lbt[:, 2, :], ALU.mult))
            own.link(vs(lbt[:, 4, :], lbt[:, 3, :], -1.0, 1.0, ALU.mult, ALU.add))
            for h in range(HEADS):
                dve.wait_ge(qf_sig, h + 1)
                c = slice(h * S, (h + 1) * S)
                vt(QD[:, h, :], QD[:, h, :], PS[:, h % 4, 0:S], ALU.mult).then_inc(qf_free, 1)
                vs(KF[:, c], KF[:, c], lbt[:, 4, h:h + 1], None, ALU.mult)
                vs(BC[:, c], BC[:, c], lbt[:, 4, h:h + 1], lbt[:, 3, h:h + 1], ALU.mult, ALU.add).then_inc(qf_lin, 1)
            for hf in range(2):
                dve.wait_ge(logf_ready, hf + 1)
                for d in range(5):
                    w = 1 << d
                    v = BC[:, hf * 1024:(hf + 1) * 1024].rearrange("p (g two w) -> p g two w", two=2, w=w)
                    op = vt(v[:, :, 1, :], v[:, :, 1, :], v[:, :, 0, w - 1:w].to_broadcast([P, 1024 // (2 * w), w]), ALU.add)
                    if d < 4:
                        own.link(op)
                    else:
                        op.then_inc(cum_ready, 1)
            for hf in range(2):
                dve.wait_ge(exps_ready, hf + 1)
                c = slice(hf * 1024, (hf + 1) * 1024)
                last_of = EX[:, c].rearrange("p (g w) -> p g w", w=CH)[:, :, CH - 1]
                nc.vector.tensor_copy(chunk_decay[:, 4 * hf:4 * hf + 4, :].rearrange("p h n -> p (h n)"), last_of)
                vt(WK1[:, c], WK1[:, c], EX[:, c], ALU.mult)
                own.link(vt(WK2[:, c], WK2[:, c], KF[:, c], ALU.mult))
                v = BC[:, c].rearrange("p (g w) -> p g w", w=CH)
                lastb = lbt_last[:, hf, :]
                own.link(nc.vector.tensor_copy(lastb, v[:, :, CH - 1]))
                vt(v, lastb.unsqueeze(2).to_broadcast([P, 32, CH]), v, ALU.subtract).then_inc(rest_ready, 1)
            for hf in range(2):
                dve.wait_ge(rest_exp, hf + 1)
                c = slice(hf * 1024, (hf + 1) * 1024)
                vt(KF[:, c], KF[:, c], EX[:, c], ALU.mult).then_inc(kend_ready, 1)
            for nh in range(2):
                for t in range(TB):
                    dve.wait_ge(g_sig, 2 * nh + t + 1)
                    v = GATE[:, t, nh * 512:(nh + 1) * 512]
                    vt(v, v, PS[:, 2 * nh + t, :], ALU.mult).then_inc(gate_ready, 1)
            dve.wait_ge(masked_zero, 1)
            dve.wait_ge(consts_ready, 6)
            SC = EX.rearrange("p (h t) -> p h t", h=HEADS)
            for h in range(HEADS):
                dve.wait_ge(score_psum, h + 1)
                nc.vector.copy_predicated(SC[:, h, :].rearrange("p (b c) -> p b c", b=TB),
                                          chunk_mask[:].unsqueeze(1).to_broadcast([P, TB, P]),
                                          PS[:, 4 + h % 4, 0:S].rearrange("p (b c) -> p b c", b=TB)).then_inc(score_ready, 1)
            for n in range(NCH - 1):
                dve.wait_ge(kv_psum, n + 1)
                if n >= 2:
                    dve.wait_ge(o_psum, n - 1)
                if n >= 1:
                    dve.wait_ge(state_ready, n)
                for h in range(HEADS):
                    kvp = PS[:, 4 + 2 * (n % 2) + h // 4, (h % 4) * P:(h % 4 + 1) * P]
                    dst = ST[:, (n + 1) % 2, h * P:(h + 1) * P]
                    if n == 0:
                        last = nc.vector.tensor_copy(dst, kvp)
                    else:
                        last = stt(out=dst, in0=ST[:, n % 2, h * P:(h + 1) * P], scalar=chunk_decay[:, h, n:n + 1],
                                   in1=kvp, op0=ALU.mult, op1=ALU.add)
                last.then_inc(state_ready, 1)
            O = BC.rearrange("p (b f) -> p b f", b=TB)
            for b in range(4):
                dve.wait_ge(o_sq, b + 1)
                own.link(red(hsum[:, 4 * b:4 * b + 4], BC[:, b * 512:(b + 1) * 512].rearrange("p (h v) -> p h v", v=P),
                             AX, ALU.add))
            vs(hsum[:], hsum[:], 1.0 / P, 1e-6, ALU.mult, ALU.add).then_inc(o_var, 1)
            dve.wait_ge(o_rstd, 1)
            for b in range(4):
                v = BC[:, b * 512:(b + 1) * 512].rearrange("p (h v) -> p h v", v=P)
                own.link(vt(v, PS[:, b, :].rearrange("p (h v) -> p h v", v=P),
                            hrstd[:, 4 * b:4 * b + 4].unsqueeze(2).to_broadcast([P, 4, P]), ALU.mult))
            vt(BC, BC, WK4[:, :], ALU.mult).then_inc(o_ready, 1)

            def add_mix(i):
                for t in range(TB):
                    for nh in range(2):
                        dve.wait_ge(mix_psum, 4 * i + 2 * t + nh + 1)
                        v = H[:, t, nh * 512:(nh + 1) * 512]
                        vt(v, v, PS[:, 2 * t + nh, :], ALU.add).then_inc(mixed, 1)
                dve.wait_ge(mixed, 4 * (i + 1))

            add_mix(0)
            norm(1)

            def expert_layer(l):
                es, xs = main_s[l], more_s[l]
                R = lambda i, w=8: rt[:, i, :, 0:w]
                wide_ = lambda a, w: a.to_broadcast([P, TB, w])

                def first_max(src, w, r_max, r_tmp, r_hot):
                    own.link(red(R(r_max, 1), src, AX, ALU.max))
                    own.link(vt(R(r_tmp, w), src, wide_(R(r_max, 1), w), ALU.is_equal))
                    own.link(stt(out=R(r_tmp, w), in0=R(r_tmp, w), scalar=-100.0,
                                 in1=slot_iota[:, 0:w].unsqueeze(1).to_broadcast([P, TB, w]), op0=ALU.mult, op1=ALU.add))
                    own.link(red(R(r_hot, 1), R(r_tmp, w), AX, ALU.min))
                    own.link(nc.vector.tensor_copy(R(15, 1), R(r_hot, 1)))
                    own.link(vt(R(r_hot, w), R(r_tmp, w), wide_(R(15, 1), w), ALU.is_equal))

                dve.wait_ge(logits_psum, l + 1)
                own.link(vt(logit, PS[:, B_XG, 0:TB * LG].rearrange("p (t n) -> p t n", t=TB),
                            rb[:, l, :].unsqueeze(1).to_broadcast([P, TB, LG]), ALU.add))
                first_max(logit[:, :, 0:G4], G4, 2, 3, 4)
                vt(R(0, G4), logit[:, :, 0:G4], wide_(R(2, 1), G4), ALU.subtract).then_inc(coarse_in, 1)
                own.link(vt(rt4, logit[:, :, G4:LG].rearrange("p t (g j) -> p t g j", g=G4),
                            R(4, G4).unsqueeze(3).to_broadcast([P, TB, G4, E8]), ALU.mult))
                own.link(red(R(5), rt4.rearrange("p t g j -> p t j g"), AX, ALU.add))
                first_max(R(5), E8, 6, 3, 7)
                own.link(stt(out=R(10), in0=R(7), scalar=NEG, in1=R(5), op0=ALU.mult, op1=ALU.add))
                first_max(R(10), E8, 11, 3, 12)
                vt(R(8, 1), R(11, 1), R(6, 1), ALU.subtract).then_inc(fine_in, 1)
                dve.wait_ge(coarse_exp, l + 1)
                own.link(red(R(2, 1), R(1, G4), AX, ALU.add))
                own.link(nc.vector.reciprocal(R(2, 1), R(2, 1)))
                dve.wait_ge(fine_exp, l + 1)
                own.link(vs(R(3, 1), R(9, 1), 1.0, None, ALU.add))
                own.link(nc.vector.reciprocal(R(3, 1), R(3, 1)))
                own.link(vt(R(13, 1), R(2, 1), R(3, 1), ALU.mult))
                own.link(vt(R(14, 1), R(13, 1), R(9, 1), ALU.mult))
                own.link(vt(R(0), R(7), R(12), ALU.add))
                own.link(vt(R(1), R(7), wide_(R(13, 1), E8), ALU.mult))
                own.link(vt(R(5), R(12), wide_(R(14, 1), E8), ALU.mult))
                own.link(vt(R(1), R(1), R(5), ALU.add))
                grp = R(4, G4).unsqueeze(3).to_broadcast([P, TB, G4, E8])
                own.link(vt(gate[:, :, 0:NE].rearrange("p t (g j) -> p t g j", g=G4), grp,
                            R(1).unsqueeze(2).to_broadcast([P, TB, G4, E8]), ALU.mult))
                own.link(nc.vector.memset(gate[:, :, NE:SW], 0.0))
                own.link(nc.vector.memset(slot[:, :, NE:SW], FAR))
                vt(member.rearrange("p t (g j) -> p t g j", g=G4), grp,
                   R(0).unsqueeze(2).to_broadcast([P, TB, G4, E8]), ALU.mult).then_inc(member_ready, 1)
                dve.wait_ge(member_ready, l + 1)
                own.link(vs(slot[:, :, 0:NE], member, -FAR, FAR, ALU.mult, ALU.add))
                dve.wait_ge(ranks_psum, l + 1)
                own.link(vt(slot[:, :, 0:NE], slot[:, :, 0:NE], PS[:, B_XG, 0:2 * NE].rearrange("p (t n) -> p t n", t=TB), ALU.add))
                own.link(red(busiest[:, 0:1], PS[:, B_XG, 2 * NE:3 * NE], AX, ALU.max))
                nc.vector.tensor_copy(busiest_i[:], busiest[:, 0:1]).then_inc(slots_ready, 1)

                def even_fills(buf, group):
                    for q in (0, 2):
                        dve.wait_ge(es.gathered, group * 4 + (q + 1))
                        for j in range(2):
                            k = 2 * q + j
                            last = vs(XE[buf][:, k, :], PS[:, B_XG, j * GRP * CAP:(j + 1) * GRP * CAP],
                                      gains[:, GA_F + 8 * l + k:GA_F + 8 * l + k + 1], None, ALU.mult)
                        last.then_inc(es.even_taken, 1)

                def build_dispatch(es_, buf, e, n):
                    nc.vector.tensor_tensor(PD[:, buf, :, 0:n, :],
                                            slot[:, :, bass.ds(e, n)].unsqueeze(3).to_broadcast([P, TB, n, CAP]),
                                            slot_iota[:].unsqueeze(1).unsqueeze(1).to_broadcast([P, TB, n, CAP]),
                                            ALU.is_equal).then_inc(es_.dispatch_built, 1)

                def times_up(es_, count):
                    dve.wait_ge(es_.silu_done, count)
                    vt(HH, HS, PS[:, B_GU, S:2 * S], ALU.mult).then_inc(es_.act_done, 1)

                def take_turned(es_, count):
                    dve.wait_ge(es_.turned, count)
                    nc.vector.tensor_copy(HG, PS[:, B_TR, :]).then_inc(es_.turned_taken, 1)

                dve.wait_ge(slots_ready, l + 1)
                build_dispatch(es, 0, 0, GRP)
                build_dispatch(es, 1, GRP, GRP)
                even_fills(0, 0)

                def step(j6, e, group, with_next):
                    times_up(es, e + 1)
                    if j6 % 3 == 0 and with_next:
                        even_fills(1 - (j6 // 3) % 2, group + 1)
                    take_turned(es, e + 1)
                    if j6 % 3 == 1 and with_next:
                        dve.wait_ge(es.gates_built, group * 4 + 4)
                        build_dispatch(es, (j6 // 3) % 2, e + 5, GRP)

                with dve.Fori(0, 5) as it:
                    for j6 in range(6):
                        step(j6, it * 6 + j6, it * 2 + j6 // 3, True)
                step(0, 30, 10, False)
                step(1, 31, 10, False)
                most = dve.value_load(busiest_i[0:1, 0:1], min_val=0, max_val=S)
                with dve.If(most > CAP):
                    with dve.Fori(0, ROUNDS - 1) as r:
                        dve.wait_ge(xs.combined, r * NE + 1)
                        vs(slot, slot, float(CAP), None, ALU.subtract).then_inc(more_shift[l], 1)
                        with dve.Fori(0, NE) as e:
                            n = r * NE + e
                            dve.wait_ge(more_shift[l], r + 1)
                            dve.wait_ge(xs.combined, n + 1)
                            build_dispatch(xs, 0, e, 1)
                            dve.wait_ge(xs.gathered, n + 1)
                            for k in range(KC):
                                last = vs(XE[0][:, k, 0:CAP], PS[:, B_XG, k * CAP:(k + 1) * CAP],
                                          gains[:, GA_F + 8 * l + k:GA_F + 8 * l + k + 1], None, ALU.mult)
                            last.then_inc(xs.even_taken, 1)
                            times_up(xs, n + 1)
                            take_turned(xs, n + 1)
                dve.wait_ge(acc_done, l + 1)
                for nh in range(2):
                    last = nc.vector.tensor_copy(H[:, 0, nh * 512:(nh + 1) * 512], PS[:, nh, :])
                last.then_inc(moe_dve, 1)

            expert_layer(0)
            norm(2)
            lv = lam[:].rearrange("p (a b) d -> p a b d", b=2)
            own.link(vt(lamt, lv[:, :, 0, :], lv[:, :, 1, :], ALU.mult))
            red(lams[:, 0:2], lamt, AX, ALU.add).then_inc(lam_dot, 1)
            dve.wait_ge(lam_exp, 1)
            own.link(vt(lams[:, 4:5], lams[:, 3:4], lams[:, 2:3], ALU.subtract))
            own.link(vs(lams[:, 5:6], lams[:, 4:5], -LAM_INIT, None, ALU.add))

            def masked(h):
                dve.wait_ge(s_psum, h + 1)
                if h >= 2:
                    dve.wait_ge(pt_psum, h - 1)
                a = att_s[:, h % 2, :]
                for m in range(2):
                    own.link(stt(out=SM[:, h % 2, m, :], in0=PS[:, 4 + 2 * (h % 2) + m, 0:3 * P], scalar=DH ** -0.5,
                                 in1=causal_neg, op0=ALU.mult, op1=ALU.add))
                for m in range(2):
                    red(a[:, 2 * m:2 * m + 1], SM[:, h % 2, m, 0:P], AX, ALU.max)
                    op = red(a[:, 2 * m + 1:2 * m + 2], SM[:, h % 2, m, P:3 * P], AX, ALU.max)
                    own.link(op)
                    vs(a[:, 4 + 2 * m:6 + 2 * m], a[:, 2 * m:2 * m + 2], -1.0, None, ALU.mult).then_inc(s_max, 1)

            def mixed_probs(h):
                dve.wait_ge(s_exp, h + 1)
                a = att_s[:, h % 2, :]
                own.link(nc.vector.reciprocal(a[:, 12:16], a[:, 8:12]))
                own.link(vs(a[:, 14:16], a[:, 14:16], lams[:, 5:6], None, ALU.mult))
                for b, c in ((0, slice(0, P)), (1, slice(P, 3 * P))):
                    own.link(vs(SM[:, h % 2, 0, c], SM[:, h % 2, 0, c], a[:, 12 + b:13 + b], None, ALU.mult))
                    op = stt(out=SM[:, h % 2, 0, c], in0=SM[:, h % 2, 1, c], scalar=a[:, 14 + b:15 + b],
                             in1=SM[:, h % 2, 0, c], op0=ALU.mult, op1=ALU.add)
                op.then_inc(p_ready, 1)

            dve.wait_ge(causal_ready, 2)
            masked(0)
            for h in range(1, HEADS):
                masked(h)
                mixed_probs(h - 1)
            mixed_probs(HEADS - 1)
            dve.wait_ge(ob_ready, HEADS)
            vs(hsum[:], hsum[:], 1.0 / P, 1e-5, ALU.mult, ALU.add).then_inc(o_var, 1)
            dve.wait_ge(o_rstd, 2)
            v = WK4[:, :].rearrange("p (g v) -> p g v", v=P)
            vt(v, v, hrstd[:].unsqueeze(2).to_broadcast([P, 16, P]), ALU.mult).then_inc(o_ready, 1)
            add_mix(1)
            norm(3)
            expert_layer(1)
            norm(4, turn=False)
            dve.wait_ge(final_gain_landed, 16)
            dve.wait_ge(xn0_ready, 5)
            vt(OUTB[:, 0, :], OUTB[:, 0, :], GROW, ALU.mult).then_inc(final_dve, 1)
            dve.wait_ge(xn1_ready, 5)
            vt(OUTB[:, 1, :], OUTB[:, 1, :], GROW, ALU.mult).then_inc(final_act, 1)


_INS = ["x", "a_norm_g", "a_w_in", "a_lb", "a_onorm_g", "a_w_out", "kv_norm_g", "w_kv", "b_norm_g", "b_w_q",
        "b_lam", "b_subln_g", "b_w_out", "ffn_norm_g", "router_g_w", "router_g_b", "router_e_w", "router_e_b",
        "expert_w_gu", "expert_w_down", "final_norm_g"]


def kernel(**inputs):
    import numpy as _np
    import concourse.bacc as _bacc
    from concourse.bass_utils import run_bass_kernel_spmd as _run

    nc = _bacc.Bacc("TRN2", target_bir_lowering=False, num_devices=1)
    arrays, args = {}, []
    for name in _INS:
        a = _np.ascontiguousarray(inputs[name])
        arrays[f"in_{name}_dram"] = a
        args.append(nc.dram_tensor(f"in_{name}_dram", a.shape, mybir.dt.from_np(a.dtype), kind="ExternalInput").ap())
    args.append(nc.dram_tensor("out_dram", (1, S, D), F32, kind="ExternalOutput").ap())
    trunk(nc, *args)
    r = _run(nc, [arrays], core_ids=[0])
    return r.results[0]["out_dram"]
```

```python
import math
from contextlib import ExitStack

import concourse.bass as bass
from concourse import mybir

F32 = mybir.dt.float32
BF16 = mybir.dt.bfloat16
I32 = mybir.dt.int32
ALU = mybir.AluOpType
ACT = mybir.ActivationFunctionType
AX = mybir.AxisListType.X

P = 128
S, D = 256, 1024
TB = S // P
KC = D // P
HEADS = 8
CH, NCH = 32, 8
G4, E8 = 4, 8
NE = G4 * E8
LG = G4 + NE
DE = 512
CAP = 64
ROUNDS = S // CAP
NS = 9
GRP = 3
SW = 36
DH = 64
LAM_INIT = 0.8 - 0.6 * math.exp(-0.3)
FAR = 1.0e4
NEG = -1.0e30

GA_A, GA_LB, GA_KV, GA_B, GA_F, GA_ON, GA_SL, NG = 0, 8, 24, 32, 40, 56, 57, 58


class Chain:

    def __init__(self, engine, sem):
        self.engine, self.sem, self.n = engine, sem, 0

    def link(self, instruction):
        instruction.then_inc(self.sem, 1)
        self.n += 1
        self.engine.wait_ge(self.sem, self.n)


def trunk(nc, x, a_norm_g, a_w_in, a_lb, a_onorm_g, a_w_out, kv_norm_g, w_kv, b_norm_g, b_w_q, b_lam,
          b_subln_g, b_w_out, ffn_norm_g, router_g_w, router_g_b, router_e_w, router_e_b,
          expert_w_gu, expert_w_down, final_norm_g, out):
    ctx = ExitStack()
    with ctx:
        def sb(name, shape, dt=F32):
            return ctx.enter_context(nc.sbuf_tensor(name, shape, dt))

        def sem(name):
            return ctx.enter_context(nc.semaphore(name))

        ring = sb("ring", [P, NS, 4096])
        H = sb("H", [P, TB, D])
        XN = sb("XN", [P, TB, D])
        XT = sb("XT", [P, KC, S])
        WK1 = sb("WK1", [P, 2048])
        WK2 = sb("WK2", [P, 2048])
        WK3 = sb("WK3", [P, 2048])
        WK4 = sb("WK4", [P, 2048])
        ident = sb("ident", [P, P])
        before = sb("before", [P, P])
        ones = sb("ones", [P, P])
        chunk_mask = sb("chunk_mask", [P, P], I32)
        slot_iota = sb("slot_iota", [P, CAP])
        gains = sb("gains", [P, NG])
        lbt = sb("lbt", [P, 5, HEADS])
        rw = sb("rw", [P, 2, KC, LG])
        rb = sb("rb", [P, 2, LG])
        lam = sb("lam", [P, 4, DH])
        lams = sb("lams", [P, 6])
        sub_gain = sb("sub_gain", [P, 1])
        ssum = sb("ssum", [P, TB])
        rstd = sb("rstd", [P, TB])
        neg_half = sb("neg_half", [P, 16])
        hsum = sb("hsum", [P, 16])
        hrstd = sb("hrstd", [P, 16])
        chunk_decay = sb("chunk_decay", [P, HEADS, NCH])
        busiest = sb("busiest", [P, 2])
        busiest_i = sb("busiest_i", [P, 1], I32)
        lbt_last = sb("lbt_last", [P, 2, 32])
        att_s = sb("att_s", [P, 3, 16])

        chunk_mask_f = WK4[:, 0:P]
        gain_rows = WK4[0:NG, P:2 * P]
        QD = WK1[:, :].rearrange("p (h t) -> p h t", h=HEADS)
        KI = WK2[:, :].rearrange("p (h t) -> p h t", h=HEADS)
        KTOK = WK3[:, :].rearrange("p (b f) -> p b f", b=TB)
        GATE = WK4[:, :].rearrange("p (b f) -> p b f", b=TB)
        KF = ring[:, 5, 0:2048]
        EX = ring[:, 5, 2048:4096]
        BC = ring[:, 6, 0:2048]
        ST = [ring[:, 6, 2048:4096].rearrange("p (n f) -> p n f", n=4), KF.rearrange("p (n f) -> p n f", n=4)]
        XT2 = WK2[:, :].rearrange("p (k t) -> p k t", k=KC)
        QT = WK1[:, :].rearrange("p (h t) -> p h t", h=HEADS)
        KT = WK3[:, :].rearrange("p (h t) -> p h t", h=HEADS)
        OB = WK4[:, :].rearrange("p (b f) -> p b f", b=TB)
        causal_neg = ring[:, 5, 0:384]
        SM = ring[:, 5, 384:384 + 2304].rearrange("p (b m c) -> p b m c", b=3, m=2)
        PT = ring[:, 5, 2688:2688 + 768].rearrange("p (b c) -> p b c", b=2)
        lamt = ring[:, 5, 3456:3456 + 2 * DH].rearrange("p (a d) -> p a d", a=2)
        XE = [WK1[:, 0:KC * GRP * CAP].rearrange("p (k c) -> p k c", k=KC),
              WK2[:, 0:KC * GRP * CAP].rearrange("p (k c) -> p k c", k=KC)]
        GD = WK3[:, 0:2 * TB * GRP * P].rearrange("p (b t e c) -> p b t e c", b=2, t=TB, e=GRP)
        PD = WK4[:, 0:TB * GRP * CAP].bitcast(BF16).rearrange("p (b t e c) -> p b t e c", b=2, t=TB, e=GRP)
        HS = WK4[:, 768:1024]
        HH = WK4[:, 1024:1280]
        HG = WK4[:, 1280:1792]
        logit = WK3[:, 1536:1608].rearrange("p (t n) -> p t n", t=TB)
        member = WK3[:, 1608:1672].rearrange("p (t n) -> p t n", t=TB)
        rt4 = WK3[:, 1672:1736].rearrange("p (t g j) -> p t g j", t=TB, g=G4)
        rt = WK3[:, 1736:1992].rearrange("p (i t w) -> p i t w", i=16, t=TB)
        gate = WK1[:, 1536:1536 + TB * SW].rearrange("p (t n) -> p t n", t=TB)
        slot = WK2[:, 1536:1536 + TB * SW].rearrange("p (t n) -> p t n", t=TB)
        XTw = XT[:, :, :].rearrange("p a b -> p (a b)")
        XNw = XN[:, :, :].rearrange("p a b -> p (a b)")
        YS = XTw[:, 0:512]
        XB = [v.bitcast(BF16).rearrange("p (t d) -> p t d", t=TB)
              for v in (XTw[:, 512:1536], XNw[:, 0:1024], XNw[:, 1024:2048])]
        SR = WK4[:, :].rearrange("p (t d) -> p t d", t=TB)
        GROW = WK3[:, 0:D]
        OUTB = ring[:, 0, 0:2048].rearrange("p (b f) -> p b f", b=TB)

        PS = ctx.enter_context(nc.psum_tensor("PS", [P, 8, 512], F32))
        B_GU, B_XG, B_Y, B_TR = 4, 5, 6, 7

        landed = [sem(f"landed{i}") for i in range(NS)]
        x_landed = sem("x_landed")
        small_landed = sem("small_landed")
        lam_landed = sem("lam_landed")
        final_gain_landed = sem("final_gain_landed")
        out_written = sem("out_written")
        consts_ready = sem("consts_ready")
        gains_psum = sem("gains_psum")
        gains_ready = sem("gains_ready")
        lb_max = sem("lb_max")
        lb_exp = sem("lb_exp")
        act_own, dve_own, pool_own = sem("act_own"), sem("dve_own"), sem("pool_own")
        squares = sem("squares")
        variances = sem("variances")
        rstd_ready = sem("rstd_ready")
        xn0_ready, xn1_ready = sem("xn0_ready"), sem("xn1_ready")
        xt_psum = sem("xt_psum")
        xt_dve, xt_act = sem("xt_dve"), sem("xt_act")
        qf_psum, qf_sig, qf_free = sem("qf_psum"), sem("qf_sig"), sem("qf_free")
        qf_lin = sem("qf_lin")
        logf_ready, cum_ready = sem("logf_ready"), sem("cum_ready")
        exps_ready, rest_ready, rest_exp = sem("exps_ready"), sem("rest_ready"), sem("rest_exp")
        kend_ready = sem("kend_ready")
        v_psum, v_ready, g_psum, g_sig, gate_ready = (sem(n) for n in ("v_psum", "v_ready", "g_psum", "g_sig", "gate_ready"))
        kt_psum, ktok_ready = sem("kt_psum"), sem("ktok_ready")
        masked_zero, score_psum, score_ready = sem("masked_zero"), sem("score_psum"), sem("score_ready")
        kv_psum, state_ready, o_psum = sem("kv_psum"), sem("state_ready"), sem("o_psum")
        o_sq, o_var, o_rstd, o_ready = sem("o_sq"), sem("o_var"), sem("o_rstd"), sem("o_ready")
        ot_psum, ot_ready = sem("ot_psum"), sem("ot_ready")
        mix_psum, mixed = sem("mix_psum"), sem("mixed")
        kproj_psum, kproj_ready = sem("kproj_psum"), sem("kproj_ready")
        qproj_psum, qproj_ready = sem("qproj_psum"), sem("qproj_ready")
        vb_psum, vb_ready = sem("vb_psum"), sem("vb_ready")
        lam_dot, lam_exp = sem("lam_dot"), sem("lam_exp")
        causal_ready = sem("causal_ready")
        s_psum, s_max, s_exp, p_ready = sem("s_psum"), sem("s_max"), sem("s_exp"), sem("p_ready")
        pt_psum, pt_ready, ob_psum, ob_ready = sem("pt_psum"), sem("pt_ready"), sem("ob_psum"), sem("ob_ready")
        logits_psum = sem("logits_psum")
        coarse_in, coarse_exp, fine_in, fine_exp = sem("coarse_in"), sem("coarse_exp"), sem("fine_in"), sem("fine_exp")
        part_made, part_taken = sem("part_made"), sem("part_taken")
        member_ready, ranks_psum, slots_ready = sem("member_ready"), sem("ranks_psum"), sem("slots_ready")

        class ExpertSems:
            def __init__(self, name):
                def s(n):
                    return sem(f"{name}_{n}")
                self.dispatch_built = s("dispatch_built")
                self.gates_built = s("gates_built")
                self.gathered = s("gathered")
                self.even_taken = s("even_taken")
                self.odd_taken = s("odd_taken")
                self.up_half = s("up_half")
                self.up_done = s("up_done")
                self.silu_done = s("silu_done")
                self.act_done = s("act_done")
                self.turned = s("turned")
                self.turned_taken = s("turned_taken")
                self.down_done = s("down_done")
                self.y_taken = s("y_taken")
                self.combined = s("combined")

        main_s = [ExpertSems(f"main{l}") for l in range(2)]
        more_s = [ExpertSems(f"more{l}") for l in range(2)]
        more_landed = [[sem(f"more{l}_landed{i}") for i in range(3)] for l in range(2)]
        more_shift = [sem(f"more{l}_shift") for l in range(2)]
        acc_done = sem("acc_done")
        moe_dve, moe_act = sem("moe_dve"), sem("moe_act")
        final_dve, final_act = sem("final_dve"), sem("final_act")

        used = [0] * NS

        def place(slot):
            used[slot] += 1
            return slot, 16 * used[slot]

        w_in = a_w_in[0].rearrange("(k p) n -> p k n", p=P)
        w_out_a = a_w_out[0].rearrange("(k p) n -> p k n", p=P)
        w_kvv = w_kv.rearrange("(k p) n -> p k n", p=P)
        w_qv = b_w_q[0].rearrange("(k p) n -> p k n", p=P)
        w_out_b = b_w_out[0].rearrange("(k p) n -> p k n", p=P)
        gu_v = [expert_w_gu[l].rearrange("e (k p) n -> p e k n", p=P) for l in range(2)]
        dn_v = [expert_w_down[l].rearrange("e (c p) n -> p e c n", p=P) for l in range(2)]

        def cols(s):
            return ring[:, s, :].rearrange("p (k n) -> p k n", k=KC)

        def rows(s):
            return ring[:, s, :].rearrange("p (k n) -> p k n", k=4)

        A_UNITS = {}
        for name, s in (("q0", 0), ("f0", 1), ("q1", 2), ("f1", 3), ("v0", 4), ("v1", 7), ("g0", 8),
                        ("g1", 4), ("o0", 7), ("o1", 8)):
            A_UNITS[name] = place(s)
        BASE = [None, None]
        ROT = [0, 6]
        BASE[0] = list(used)
        for u in range(3 * NE):
            used[(u + ROT[0]) % NS] += 1
        B_UNITS = {}
        for name, s in (("k0", 6), ("k1", 7), ("v0", 8), ("v1", 0), ("q0", 1), ("q1", 2), ("o0", 3), ("o1", 4)):
            B_UNITS[name] = place(s)
        BASE[1] = list(used)

        def unit_slot(layer, e, i):
            return (3 * (e % 3) + i + ROT[layer]) % NS

        def unit_count(layer, e, i, third):
            return (third + BASE[layer][unit_slot(layer, e, i)] + 1) * 16

        block = ctx.enter_context(nc.Block())

        @block.sync
        def _(sp):
            for b in range(TB):
                sp.dma_start(H[:, b, :], x[0, b * P:(b + 1) * P, :]).then_inc(x_landed, 16)
            for dst, n, src in ((GA_A, 8, a_norm_g[0]), (GA_LB, 8, a_lb[0]), (GA_LB + 8, 8, a_lb[1]),
                                (GA_KV, 8, kv_norm_g), (GA_B, 8, b_norm_g[0]), (GA_F, 8, ffn_norm_g[0]),
                                (GA_F + 8, 8, ffn_norm_g[1]), (GA_ON, 1, a_onorm_g[0]), (GA_SL, 1, b_subln_g[0])):
                sp.dma_start(gain_rows[dst:dst + n, :], src.rearrange("(k p) -> k p", p=P)).then_inc(small_landed, 16)

            def unit(table, name, dst, src):
                s, _ = table[name]
                sp.dma_start(dst(s), src).then_inc(landed[s], 16)

            for name, c in (("q0", 0), ("f0", 2), ("q1", 1), ("f1", 3), ("v0", 4), ("v1", 5), ("g0", 6)):
                unit(A_UNITS, name, cols, w_in[:, :, c * 512:(c + 1) * 512])
            for l in range(2):
                sp.dma_start(rw[:, l, :, 0:G4], router_g_w[l].rearrange("(k p) n -> p k n", p=P)).then_inc(lam_landed, 16)
                sp.dma_start(rw[:, l, :, G4:LG], router_e_w[l].rearrange("(k p) n -> p k n", p=P)).then_inc(lam_landed, 16)
                sp.dma_start(rb[:, l, 0:G4], router_g_b[l].partition_broadcast(P)).then_inc(lam_landed, 16)
                sp.dma_start(rb[:, l, G4:LG], router_e_b[l].partition_broadcast(P)).then_inc(lam_landed, 16)
            sp.dma_start(lam[:], b_lam[0].partition_broadcast(P)).then_inc(lam_landed, 16)
            sp.wait_ge(v_psum, 2)
            unit(A_UNITS, "g1", cols, w_in[:, :, 7 * 512:8 * 512])
            sp.wait_ge(v_psum, 4)
            unit(A_UNITS, "o0", rows, w_out_a[:, 0:4, :])
            sp.wait_ge(g_psum, 2)
            unit(A_UNITS, "o1", rows, w_out_a[:, 4:8, :])

            def expert_unit(l, e, j, i):
                s = unit_slot(l, j, i)
                if i < 2:
                    src = gu_v[l][:, bass.ds(e, 1), 4 * i:4 * i + 4, :]
                else:
                    src = dn_v[l][:, bass.ds(e, 1), :, :]
                sp.dma_start(ring[:, s, :].rearrange("p (e k n) -> p e k n", e=1, k=4), src).then_inc(landed[s], 16)

            def expert_layer(l, first_waits):
                es, xs = main_s[l], more_s[l]
                for u in range(9):
                    for s_, v_ in first_waits.get(u, ()):
                        sp.wait_ge(s_, v_)
                    expert_unit(l, u // 3, u // 3, u % 3)
                freed = (es.up_half, es.up_done, es.down_done)
                with sp.Fori(0, NE // 3 - 1) as g:
                    for j in range(3):
                        for i in range(3):
                            sp.wait_ge(freed[i], g * 3 + (j + 1))
                            expert_unit(l, g * 3 + (3 + j), j, i)
                for e in range(NE - NE % 3, NE):
                    for i in range(3):
                        sp.wait_ge(freed[i], e - 2)
                        expert_unit(l, e, e % 3, i)
                sp.wait_ge(slots_ready, l + 1)
                most = sp.value_load(busiest_i[0:1, 0:1], min_val=0, max_val=S)
                with sp.If(most > CAP):
                    sp.wait_ge(es.combined, NE)
                    with sp.Fori(0, (ROUNDS - 1)) as r:
                        with sp.Fori(0, NE) as e:
                            for i in range(3):
                                sp.wait_ge(xs.combined, r * NE + e + 1)
                                src = gu_v[l][:, bass.ds(e, 1), 4 * i:4 * i + 4, :] if i < 2 else dn_v[l][:, bass.ds(e, 1), :, :]
                                sp.dma_start(ring[:, i, :].rearrange("p (e k n) -> p e k n", e=1, k=4),
                                             src).then_inc(more_landed[l][i], 16)
                    sp.wait_ge(xs.combined, (ROUNDS - 1) * NE + 1)

            expert_layer(0, {0: [(qf_psum, 4)], 2: [(qf_psum, 8)], 4: [(g_psum, 4)], 5: [(ot_psum, 4)], 7: [(mix_psum, 4)]})
            es = main_s[0]
            last = {6: (es.up_half, 30), 7: (es.up_done, 30), 8: (es.down_done, 30), 0: (es.up_half, 31),
                    1: (es.up_done, 31), 2: (es.down_done, 31), 3: (es.up_half, 32), 4: (es.up_done, 32)}
            for name, dst, src in (("k0", cols, w_kvv[:, :, 0:512]), ("k1", cols, w_kvv[:, :, 512:1024]),
                                   ("v0", cols, w_kvv[:, :, 1024:1536]), ("v1", cols, w_kvv[:, :, 1536:2048]),
                                   ("q0", cols, w_qv[:, :, 0:512]), ("q1", cols, w_qv[:, :, 512:1024]),
                                   ("o0", rows, w_out_b[:, 0:4, :]), ("o1", rows, w_out_b[:, 4:8, :])):
                sp.wait_ge(*last[B_UNITS[name][0]])
                unit(B_UNITS, name, dst, src)
            expert_layer(1, {0: [(kproj_psum, 2)], 1: [(kproj_psum, 4)], 2: [(vb_psum, 2)], 3: [(vb_psum, 4)],
                             4: [(qproj_psum, 2)], 5: [(qproj_psum, 4)], 6: [(mix_psum, 8)], 8: [(ot_psum, 8)]})
            sp.wait_ge(acc_done, 2)
            sp.dma_start(GROW, final_norm_g.partition_broadcast(P)).then_inc(final_gain_landed, 16)
            sp.wait_ge(final_dve, 1)
            sp.dma_start(out[0, 0:P, :], OUTB[:, 0, :]).then_inc(out_written, 16)
            sp.wait_ge(final_act, 1)
            sp.dma_start(out[0, P:S, :], OUTB[:, 1, :]).then_inc(out_written, 16)
            sp.wait_ge(out_written, 32)

        @block.gpsimd
        def _(pool):
            own = Chain(pool, pool_own)
            gp = nc.gpsimd
            own.link(gp.memset(ident[:], 0.0))
            gp.affine_select(out=ident[:], in_=ident[:], compare_op=ALU.not_equal, fill=1.0, base=0,
                             pattern=[[-1, P]], channel_multiplier=1).then_inc(consts_ready, 1)
            gp.memset(neg_half[:], -0.5).then_inc(consts_ready, 1)
            gp.memset(ones[:], 1.0).then_inc(consts_ready, 1)
            pool.wait_ge(consts_ready, 3)
            gp.affine_select(out=before[:], in_=ones[:], compare_op=ALU.is_ge, fill=0.0, base=-1,
                             pattern=[[1, P]], channel_multiplier=-1).then_inc(consts_ready, 1)
            gp.iota(slot_iota[:], [[1, CAP]], base=0, channel_multiplier=0,
                    allow_small_or_imprecise_dtypes=True).then_inc(consts_ready, 1)
            own.link(gp.affine_select(out=chunk_mask_f, in_=ones[:], compare_op=ALU.is_ge, fill=0.0, base=0,
                                      pattern=[[1, P]], channel_multiplier=-1))
            cm = chunk_mask_f.rearrange("p (b c) -> p b c", c=CH)
            own.link(gp.affine_select(out=cm, in_=cm, compare_op=ALU.is_ge, fill=0.0, base=0,
                                      pattern=[[-CH, P // CH], [0, CH]], channel_multiplier=1))
            gp.tensor_copy(chunk_mask[:], chunk_mask_f).then_inc(consts_ready, 1)

            def norm(i):
                pool.wait_ge(variances, i + 1)
                gp.tensor_tensor(rstd[:], ssum[:], neg_half[:, 0:TB], ALU.pow).then_inc(rstd_ready, 1)

            def head_norm(i):
                pool.wait_ge(o_var, i + 1)
                gp.tensor_tensor(hrstd[:], hsum[:], neg_half[:], ALU.pow).then_inc(o_rstd, 1)

            def build_gates(es, buf, e, n, count):
                pool.wait_ge(es.dispatch_built, count)
                for t in range(TB):
                    for dup in range(2):
                        gp.tensor_tensor(GD[:, buf, t, 0:n, dup * CAP:(dup + 1) * CAP], PD[:, buf, t, 0:n, :],
                                         gate[:, t, bass.ds(e, n)].unsqueeze(2).to_broadcast([P, n, CAP]),
                                         ALU.mult).then_inc(es.gates_built, 1)

            def expert_layer(l):
                es, xs = main_s[l], more_s[l]
                pool.wait_ge(part_made, 3 * l + 1)
                gp.tensor_tensor(SR, XN[:, :, :], XB[0], ALU.subtract).then_inc(part_taken, 1)
                pool.wait_ge(part_made, 3 * l + 2)
                gp.tensor_tensor(SR, SR, XB[1], ALU.subtract).then_inc(part_taken, 1)
                pool.wait_ge(slots_ready, l + 1)
                build_gates(es, 0, 0, GRP, 1)
                build_gates(es, 1, GRP, GRP, 2)
                with pool.Fori(0, 4) as it:
                    for b in range(2):
                        pool.wait_ge(es.turned, it * 6 + (3 * b + 3))
                        build_gates(es, b, it * 6 + (6 + 3 * b), GRP, it * 2 + (b + 3))
                pool.wait_ge(es.turned, 27)
                build_gates(es, 0, 30, GRP, 11)
                most = pool.value_load(busiest_i[0:1, 0:1], min_val=0, max_val=S)
                with pool.If(most > CAP):
                    with pool.Fori(0, ROUNDS - 1) as r:
                        with pool.Fori(0, NE) as e:
                            build_gates(xs, 0, e, 1, r * NE + e + 1)

            norm(0)
            pool.wait_ge(kend_ready, 2)
            gp.memset(EX, 0.0).then_inc(masked_zero, 1)
            head_norm(0)
            norm(1)
            expert_layer(0)
            norm(2)
            pool.wait_ge(moe_dve, 1)
            own.link(gp.memset(causal_neg, 0.0))
            for c0 in (0, 256):
                gp.affine_select(out=causal_neg[:, c0:c0 + P], in_=causal_neg[:, c0:c0 + P], compare_op=ALU.is_ge,
                                 fill=NEG, base=0, pattern=[[-1, P]], channel_multiplier=1).then_inc(causal_ready, 1)
            head_norm(1)
            norm(3)
            expert_layer(1)
            norm(4)

        @block.tensor
        def _(pe):
            mm, tr = nc.tensor.matmul, nc.tensor.transpose

            def norm(i):
                if i == 0:
                    pe.wait_ge(consts_ready, 1)
                pe.wait_ge(xn0_ready, i + 1)
                pe.wait_ge(xn1_ready, i + 1)
                for b in range(4):
                    for j in range(2):
                        k = 2 * b + j
                        for t in range(TB):
                            last = tr(PS[:, 4 + b, j * S + t * P:j * S + (t + 1) * P], XN[:, t, k * P:(k + 1) * P], ident[:])
                    last.then_inc(xt_psum, 1)

            def token_major(bank, src, t, w, sem_):
                for k in range(KC):
                    last = mm(PS[:, bank, :], src[:, k, t * P:(t + 1) * P], w(k), start=(k == 0), stop=(k == KC - 1))
                last.then_inc(sem_, 1)

            def mix_out(i, units):
                pe.wait_ge(ot_ready, 4 * (i + 1))
                for n in ("o0", "o1"):
                    pe.wait_ge(landed[units[n][0]], units[n][1])
                for t in range(TB):
                    for nh in range(2):
                        token_major(2 * t + nh, XT, t,
                                    lambda k: rows(units["o0" if k < 4 else "o1"][0])[:, k % 4, nh * 512:(nh + 1) * 512],
                                    mix_psum)

            def turn_heads(src, i):
                for b in range(4):
                    for j in range(2):
                        h = 2 * b + j
                        for t in range(TB):
                            last = tr(PS[:, 4 + b, j * S + t * P:j * S + (t + 1) * P], src[:, t, h * P:(h + 1) * P], ident[:])
                    last.then_inc(ot_psum, 1)

            pe.wait_ge(consts_ready, 1)
            pe.wait_ge(small_landed, 16 * 9)
            tr(PS[:, 0, 0:NG], gain_rows, ident[0:NG, 0:NG]).then_inc(gains_psum, 1)
            norm(0)
            pe.wait_ge(gains_ready, 1)
            pe.wait_ge(xt_dve, 4)
            pe.wait_ge(xt_act, 4)
            for h in range(HEADS):
                if h % 4 == 0:
                    for n in ("q", "f"):
                        pe.wait_ge(landed[A_UNITS[f"{n}{h // 4}"][0]], A_UNITS[f"{n}{h // 4}"][1])
                if h >= 4:
                    pe.wait_ge(qf_free, h - 3)
                for j, n in enumerate(("q", "f")):
                    w = cols(A_UNITS[f"{n}{h // 4}"][0])
                    c = (h % 4) * P
                    for k in range(KC):
                        last = mm(PS[:, h % 4, j * S:(j + 1) * S], w[:, k, c:c + P], XT[:, k, :],
                                  start=(k == 0), stop=(k == KC - 1))
                last.then_inc(qf_psum, 1)
            for nh in range(2):
                pe.wait_ge(landed[A_UNITS[f"v{nh}"][0]], A_UNITS[f"v{nh}"][1])
                for t in range(TB):
                    token_major(4 + 2 * nh + t, XT, t, lambda k: cols(A_UNITS[f"v{nh}"][0])[:, k, :], v_psum)
            pe.wait_ge(qf_free, HEADS)
            for nh in range(2):
                pe.wait_ge(landed[A_UNITS[f"g{nh}"][0]], A_UNITS[f"g{nh}"][1])
                for t in range(TB):
                    token_major(2 * nh + t, XT, t, lambda k: cols(A_UNITS[f"g{nh}"][0])[:, k, :], g_psum)
            pe.wait_ge(v_ready, 4)
            pe.wait_ge(kend_ready, 2)
            KFh = KF.rearrange("p (h t) -> p h t", h=HEADS)
            for t in range(TB):
                for hh in range(2):
                    for h in range(4 * hh, 4 * hh + 4):
                        last = tr(PS[:, 4 + 2 * t + hh, (h % 4) * P:(h % 4 + 1) * P], KFh[:, h, t * P:(t + 1) * P], ident[:])
                    last.then_inc(kt_psum, 1)
            pe.wait_ge(ktok_ready, 4)
            SC = EX.rearrange("p (h t) -> p h t", h=HEADS)
            VA = XN

            def intra(t, nh):
                for hh in range(4):
                    h = 4 * nh + hh
                    mm(PS[:, 2 * t + nh, hh * P:(hh + 1) * P], SC[:, h, t * P:(t + 1) * P], VA[:, t, h * P:(h + 1) * P],
                       start=(hh == 0), stop=True, skip_group_check=True)

            for h in range(HEADS):
                if h >= 4:
                    pe.wait_ge(score_ready, h - 3)
                for t in range(TB):
                    last = mm(PS[:, 4 + h % 4, t * P:(t + 1) * P], KI[:, h, t * P:(t + 1) * P], QD[:, h, t * P:(t + 1) * P],
                              start=True, stop=True)
                last.then_inc(score_psum, 1)
            pe.wait_ge(score_ready, HEADS)
            pe.wait_ge(gate_ready, 4)

            def chunk_kv(t, hh):
                for h in range(4 * hh, 4 * hh + 4):
                    for c in range(4 - t):
                        last = mm(PS[:, 4 + c, (h % 4) * P:(h % 4 + 1) * P],
                                  KTOK[c * CH:(c + 1) * CH, t, h * P:(h + 1) * P], VA[c * CH:(c + 1) * CH, t, h * P:(h + 1) * P],
                                  start=True, stop=True, tile_position=(c * CH, 0))
                last.then_inc(kv_psum, 1)

            def inter(t, hh):
                for h in range(4 * hh, 4 * hh + 4):
                    for c in range(1 - t, 4):
                        n = 4 * t + c
                        last = mm(PS[c * CH:(c + 1) * CH, 2 * t + hh, (h % 4) * P:(h % 4 + 1) * P],
                                  QD[:, h, n * CH:(n + 1) * CH], ST[hh][:, c, (h % 4) * P:(h % 4 + 1) * P],
                                  start=False, stop=True, skip_group_check=True, tile_position=(0, c * CH))
                last.then_inc(o_psum, 1)

            quads = [(0, 0), (0, 1), (1, 0), (1, 1)]
            chunk_kv(0, 0)
            for t in range(TB):
                for nh in range(2):
                    intra(t, nh)
            for i, (t, hh) in enumerate(quads):
                pe.wait_ge(state_ready, i + 1)
                if i + 1 < 4:
                    chunk_kv(*quads[i + 1])
                inter(t, hh)
            pe.wait_ge(o_ready, 1)
            turn_heads(BC.rearrange("p (b f) -> p b f", b=TB), 0)
            mix_out(0, A_UNITS)

            def gather_fill(es, pd, chunks, width, bank):
                for j, k in enumerate(chunks):
                    for i in range(TB * 3):
                        t, part = i % TB, i // TB
                        last = mm(PS[:, bank, j * width:(j + 1) * width], XB[part][:, t, k * P:(k + 1) * P], pd[:, t],
                                  start=(i == 0), stop=(i == TB * 3 - 1))
                last.then_inc(es.gathered, 1)

            def gather(es, buf, group):
                pe.wait_ge(es.dispatch_built, group + 1)
                pd = PD[:, buf, :, :, :].rearrange("p t e c -> p t (e c)")
                gather_fill(es, pd, (0, 1), GRP * CAP, B_XG)
                gather_fill(es, pd, (2, 3), GRP * CAP, B_Y)
                pe.wait_ge(es.even_taken, group * 2 + 1)
                gather_fill(es, pd, (4, 5), GRP * CAP, B_XG)
                pe.wait_ge(es.odd_taken, group * 2 + 1)
                gather_fill(es, pd, (6, 7), GRP * CAP, B_Y)

            def up(es, xe, wa, wb, wait_a, wait_b):
                for i, (w, wait) in enumerate(((wa, wait_a), (wb, wait_b))):
                    pe.wait_ge(*wait)
                    for kk in range(4):
                        k = 4 * i + kk
                        cw = w[:, kk, :].rearrange("p (a h f) -> p a h f", a=2, h=2)
                        for half in range(2):
                            last = mm(PS[CAP * half:CAP * (half + 1), B_GU, :].rearrange("p (a f) -> p a f", a=2), xe(k),
                                      cw[:, :, half, :], start=(k == 0), stop=(k == KC - 1), tile_position=(0, CAP * half))
                    last.then_inc(es.up_half if i == 0 else es.up_done, 1)

            def turn(es, gd, count, gates_count):
                pe.wait_ge(es.gates_built, gates_count)
                pe.wait_ge(es.act_done, count)
                for j in range(2):
                    tr(PS[:, B_TR, j * P:(j + 1) * P], HH[:, j * P:(j + 1) * P], ident[:])
                for t in range(TB):
                    last = tr(PS[:, B_TR, (2 + t) * P:(3 + t) * P], gd[:, t], ident[:])
                last.then_inc(es.turned, 1)

            def down(es, w, wait, count):
                pe.wait_ge(*wait)
                pe.wait_ge(es.turned_taken, count * 2 - 1)
                for c in range(4):
                    half, j = c // 2, c % 2
                    for nh in range(2):
                        last = mm(PS[CAP * nh:CAP * (nh + 1), B_Y, :], HG[:, j * P + half * CAP:j * P + (half + 1) * CAP],
                                  w[:, c, nh * 512:(nh + 1) * 512], start=(c == 0), stop=(c == 3),
                                  tile_position=(0, CAP * nh))
                last.then_inc(es.down_done, 1)

            def combine(es, count):
                pe.wait_ge(es.y_taken, count)
                pe.wait_ge(es.turned_taken, count * 2)
                for t in range(TB):
                    for nh in range(2):
                        last = mm(PS[:, 2 * t + nh, :], HG[CAP * nh:CAP * (nh + 1), (2 + t) * P:(3 + t) * P],
                                  YS[CAP * nh:CAP * (nh + 1), :], start=False, stop=True, skip_group_check=True,
                                  tile_position=(CAP * nh, 0))
                last.then_inc(es.combined, 1)

            def expert_layer(l):
                es, xs = main_s[l], more_s[l]
                pe.wait_ge(xt_dve, 4 * l + 8 + 4 * l)
                pe.wait_ge(xt_act, 4 * l + 8 + 4 * l)
                if l == 0:
                    pe.wait_ge(lam_landed, 16 * 9)
                for t in range(TB):
                    for k in range(KC):
                        last = mm(PS[:, B_XG, t * LG:(t + 1) * LG], XT[:, k, t * P:(t + 1) * P], rw[:, l, k, :],
                                  start=(k == 0), stop=(k == KC - 1))
                last.then_inc(logits_psum, 1)
                for t in range(TB):
                    for nh in range(2):
                        mm(PS[:, 2 * t + nh, :], ident[:], H[:, t, nh * 512:(nh + 1) * 512], start=True, stop=True)
                pe.wait_ge(member_ready, l + 1)
                if l == 0:
                    pe.wait_ge(consts_ready, 5)
                mm(PS[:, B_XG, 0:NE], before[:], member[:, 0, :], start=True, stop=True)
                mm(PS[:, B_XG, NE:2 * NE], ones[:], member[:, 0, :], start=True, stop=False)
                mm(PS[:, B_XG, NE:2 * NE], before[:], member[:, 1, :], start=False, stop=True)
                mm(PS[:, B_XG, 2 * NE:3 * NE], ones[:], member[:, 0, :], start=True, stop=False)
                mm(PS[:, B_XG, 2 * NE:3 * NE], ones[:], member[:, 1, :], start=False, stop=True).then_inc(ranks_psum, 1)
                pe.wait_ge(slots_ready, l + 1)
                pe.wait_ge(part_made, 3 * (l + 1))
                gather(es, 0, 0)

                def begin(j6, e, third):
                    buf, jj = (j6 // 3) % 2, j6 % 3
                    if jj == 0:
                        pe.wait_ge(es.even_taken, third * 2 + 2)
                        pe.wait_ge(es.odd_taken, third * 2 + 2)
                    s0, s1 = unit_slot(l, j6, 0), unit_slot(l, j6, 1)
                    up(es, lambda k: XE[buf][:, k, jj * CAP:(jj + 1) * CAP], rows(s0), rows(s1),
                       (landed[s0], unit_count(l, j6, 0, third)), (landed[s1], unit_count(l, j6, 1, third)))

                def step(j6, e, third, last=False, next_gather=True):
                    buf, jj = (j6 // 3) % 2, j6 % 3
                    turn(es, GD[:, buf, :, jj, :], e + 1, third * 4 + 4)
                    if jj == 0 and next_gather:
                        pe.wait_ge(es.odd_taken, third * 2 + 4)
                    s2 = unit_slot(l, j6, 2)
                    down(es, rows(s2), (landed[s2], unit_count(l, j6, 2, third)), e + 1)
                    if not last:
                        begin((j6 + 1) % 6, e + 1, third + (1 if jj == 2 else 0))
                    combine(es, e + 1)
                    if jj == 2 and next_gather:
                        gather(es, buf, third + 2)

                begin(0, 0, 0)
                gather(es, 1, 1)
                with pe.Fori(0, 4) as it:
                    for j6 in range(6):
                        step(j6, it * 6 + j6, it * 2 + j6 // 3)
                for e in range(24, NE):
                    step(e % 6, e, e // 3, last=(e == NE - 1), next_gather=(e // 3 < 9 if e % 3 == 2 else e // 3 < 10))

                most = pe.value_load(busiest_i[0:1, 0:1], min_val=0, max_val=S)
                with pe.If(most > CAP):
                    pe.wait_ge(es.combined, NE)
                    pe.sem_inc(xs.combined, 1)
                    with pe.Fori(0, ROUNDS - 1) as r:
                        with pe.Fori(0, NE) as e:
                            n = r * NE + e
                            pe.wait_ge(xs.dispatch_built, n + 1)
                            gather_fill(xs, PD[:, 0, :, 0, :], range(KC), CAP, B_XG)
                            pe.wait_ge(xs.even_taken, n + 1)
                            up(xs, lambda k: XE[0][:, k, 0:CAP], rows(0), rows(1),
                               (more_landed[l][0], n * 16 + 16), (more_landed[l][1], n * 16 + 16))
                            turn(xs, GD[:, 0, :, 0, :], n + 1, (n + 1) * 4)
                            down(xs, rows(2), (more_landed[l][2], n * 16 + 16), n + 1)
                            combine(xs, n + 1)
                    pe.wait_ge(xs.combined, (ROUNDS - 1) * NE + 1)
                pe.wait_ge(es.combined, NE)
                pe.sem_inc(acc_done, 1)

            norm(1)
            expert_layer(0)

            norm(2)
            pe.wait_ge(moe_dve, 1)
            pe.wait_ge(moe_act, 1)
            pe.wait_ge(xt_dve, 12)
            pe.wait_ge(xt_act, 12)
            for h in range(HEADS):
                if h % 4 == 0:
                    pe.wait_ge(landed[B_UNITS[f"k{h // 4}"][0]], B_UNITS[f"k{h // 4}"][1])
                w = cols(B_UNITS[f"k{h // 4}"][0])
                for k in range(KC):
                    last = mm(PS[:, h // 2, (h % 2) * S:(h % 2 + 1) * S], w[:, k, (h % 4) * P:(h % 4 + 1) * P], XT[:, k, :],
                              start=(k == 0), stop=(k == KC - 1))
                if h % 2:
                    last.then_inc(kproj_psum, 1)
            for nh in range(2):
                pe.wait_ge(landed[B_UNITS[f"v{nh}"][0]], B_UNITS[f"v{nh}"][1])
                for t in range(TB):
                    token_major(4 + 2 * nh + t, XT, t, lambda k: cols(B_UNITS[f"v{nh}"][0])[:, k, :], vb_psum)
            pe.wait_ge(kproj_ready, 4)
            for h in range(HEADS):
                if h % 4 == 0:
                    pe.wait_ge(landed[B_UNITS[f"q{h // 4}"][0]], B_UNITS[f"q{h // 4}"][1])
                w = cols(B_UNITS[f"q{h // 4}"][0])
                for k in range(KC):
                    last = mm(PS[:, h // 2, (h % 2) * S:(h % 2 + 1) * S], w[:, k, (h % 4) * P:(h % 4 + 1) * P], XT2[:, k, :],
                              start=(k == 0), stop=(k == KC - 1))
                if h % 2:
                    last.then_inc(qproj_psum, 1)
            pe.wait_ge(vb_ready, 4)
            pe.wait_ge(qproj_ready, 4)

            def scores(h):
                if h >= 2:
                    pe.wait_ge(s_max, 2 * (h - 1))
                for m in range(2):
                    r, bank = DH * m, 4 + 2 * (h % 2) + m
                    mm(PS[:, bank, 0:P], QT[r:r + DH, h, 0:P], KT[r:r + DH, h, 0:P], start=True, stop=True,
                       tile_position=(r, 0))
                    last = mm(PS[:, bank, P:3 * P], QT[r:r + DH, h, P:S], KT[r:r + DH, h, :], start=True, stop=True,
                              tile_position=(r, 0))
                last.then_inc(s_psum, 1)

            def turn_probs(h):
                pe.wait_ge(p_ready, h + 1)
                if h >= 2:
                    pe.wait_ge(pt_ready, h - 1)
                for j in range(3):
                    last = tr(PS[:, h % 2, j * P:(j + 1) * P], SM[:, h % 3, 0, j * P:(j + 1) * P], ident[:])
                last.then_inc(pt_psum, 1)

            def values(h):
                pe.wait_ge(pt_ready, h + 1)
                if h >= 2:
                    pe.wait_ge(ob_ready, h - 1)
                v = XN[:, :, h * P:(h + 1) * P]
                mm(PS[:, 2 + h % 2, 0:P], PT[:, h % 2, 0:P], v[:, 0, :], start=True, stop=True)
                mm(PS[:, 2 + h % 2, P:S], PT[:, h % 2, P:2 * P], v[:, 0, :], start=True, stop=False)
                mm(PS[:, 2 + h % 2, P:S], PT[:, h % 2, 2 * P:3 * P], v[:, 1, :], start=False, stop=True).then_inc(ob_psum, 1)

            for i in range(HEADS + 2):
                if i < HEADS:
                    scores(i)
                if 1 <= i <= HEADS:
                    turn_probs(i - 1)
                if i >= 2:
                    values(i - 2)
            pe.wait_ge(o_ready, 2)
            turn_heads(OB, 1)
            pe.wait_ge(ob_ready, HEADS)
            mix_out(1, B_UNITS)
            norm(3)
            expert_layer(1)

        @block.scalar
        def _(act):
            own = Chain(act, act_own)
            af = nc.scalar.activation

            def norm(i, turn=True, second=None):
                for t in range(TB):
                    af(XN[:, t, :], H[:, t, :], ACT.Square, accum_out=ssum[:, t:t + 1]).then_inc(squares, 1)
                act.wait_ge(rstd_ready, i + 1)
                dst = XN[:, 1, :] if turn else OUTB[:, 1, :]
                af(dst, H[:, 1, :], ACT.Identity, scale=rstd[:, 1:2]).then_inc(xn1_ready, 1)
                if not turn:
                    return
                if i == 0:
                    act.wait_ge(gains_ready, 1)
                for b in (2, 3):
                    act.wait_ge(xt_psum, 4 * i + b + 1)
                    for j in range(2):
                        k = 2 * b + j
                        g = {0: GA_A, 1: GA_F, 2: GA_KV, 3: GA_F + 8}[i]
                        if i == 2:
                            own.link(af(XT2[:, k, :], PS[:, 4 + b, j * S:(j + 1) * S], ACT.Identity,
                                        scale=gains[:, GA_B + k:GA_B + k + 1]))
                        af(XT[:, k, :], PS[:, 4 + b, j * S:(j + 1) * S], ACT.Identity,
                           scale=gains[:, g + k:g + k + 1]).then_inc(xt_act, 1)

            act.wait_ge(x_landed, 32)
            norm(0)
            act.wait_ge(lb_max, 1)
            af(lbt[:, 0:2, :], lbt[:, 0:2, :], ACT.Exp).then_inc(lb_exp, 1)
            for h in range(HEADS):
                act.wait_ge(qf_psum, h + 1)
                af(QD[:, h, :], PS[:, h % 4, 0:S], ACT.Sigmoid)
                af(BC[:, h * S:(h + 1) * S], PS[:, h % 4, S:2 * S], ACT.Sigmoid)
                af(KF[:, h * S:(h + 1) * S], PS[:, h % 4, S:2 * S], ACT.Sigmoid, scale=-1.0).then_inc(qf_sig, 1)
            for hf in range(2):
                act.wait_ge(qf_lin, 4 * (hf + 1))
                c = slice(hf * 1024, (hf + 1) * 1024)
                af(BC[:, c], BC[:, c], ACT.Ln).then_inc(logf_ready, 1)
            for hf in range(2):
                act.wait_ge(cum_ready, hf + 1)
                c = slice(hf * 1024, (hf + 1) * 1024)
                af(EX[:, c], BC[:, c], ACT.Exp)
                af(WK2[:, c], BC[:, c], ACT.Exp, scale=-1.0).then_inc(exps_ready, 1)
            for hf in range(2):
                act.wait_ge(rest_ready, hf + 1)
                c = slice(hf * 1024, (hf + 1) * 1024)
                af(EX[:, c], BC[:, c], ACT.Exp).then_inc(rest_exp, 1)
            for nh in range(2):
                for t in range(TB):
                    act.wait_ge(v_psum, 2 * nh + t + 1)
                    nc.scalar.copy(XN[:, t, nh * 512:(nh + 1) * 512], PS[:, 4 + 2 * nh + t, :]).then_inc(v_ready, 1)
            for nh in range(2):
                for t in range(TB):
                    act.wait_ge(g_psum, 2 * nh + t + 1)
                    af(GATE[:, t, nh * 512:(nh + 1) * 512], PS[:, 2 * nh + t, :], ACT.Sigmoid).then_inc(g_sig, 1)
            for t in range(TB):
                for hh in range(2):
                    act.wait_ge(kt_psum, 2 * t + hh + 1)
                    nc.scalar.copy(KTOK[:, t, hh * 512:(hh + 1) * 512], PS[:, 4 + 2 * t + hh, :]).then_inc(ktok_ready, 1)
            act.wait_ge(o_psum, 4)
            for b in range(4):
                af(BC[:, b * 512:(b + 1) * 512], PS[:, b, :], ACT.Square).then_inc(o_sq, 1)

            def turned_heads(i, gain, banks):
                for b in banks:
                    act.wait_ge(ot_psum, 4 * i + b + 1)
                    af(XT[:, 2 * b:2 * b + 2, :], PS[:, 4 + b, :].rearrange("p (a t) -> p a t", a=2), ACT.Identity,
                       scale=gain).then_inc(ot_ready, 1)

            turned_heads(0, gains[:, GA_ON:GA_ON + 1], range(4))

            def expert_layer(l):
                es, xs = main_s[l], more_s[l]
                act.wait_ge(logits_psum, l + 1)
                nc.scalar.copy(XB[0], XN[:, :, :]).then_inc(part_made, 1)
                act.wait_ge(coarse_in, l + 1)
                af(rt[:, 1, :, 0:G4], rt[:, 0, :, 0:G4], ACT.Exp).then_inc(coarse_exp, 1)
                act.wait_ge(fine_in, l + 1)
                af(rt[:, 9, :, 0:1], rt[:, 8, :, 0:1], ACT.Exp).then_inc(fine_exp, 1)
                for i in (1, 2):
                    act.wait_ge(part_taken, 2 * l + i)
                    nc.scalar.copy(XB[i], SR).then_inc(part_made, 1)

                def odd_fills(buf, group):
                    for q in (1, 3):
                        act.wait_ge(es.gathered, group * 4 + (q + 1))
                        for j in range(2):
                            k = 2 * q + j
                            last = af(XE[buf][:, k, :], PS[:, B_Y, j * GRP * CAP:(j + 1) * GRP * CAP], ACT.Identity,
                                      scale=gains[:, GA_F + 8 * l + k:GA_F + 8 * l + k + 1])
                        last.then_inc(es.odd_taken, 1)

                def silu(es_, count):
                    act.wait_ge(es_.up_done, count)
                    af(HS, PS[:, B_GU, 0:S], ACT.Silu).then_inc(es_.silu_done, 1)

                def take_y(es_, count):
                    act.wait_ge(es_.down_done, count)
                    nc.scalar.copy(YS, PS[:, B_Y, :]).then_inc(es_.y_taken, 1)

                odd_fills(0, 0)
                silu(es, 1)
                odd_fills(1, 1)

                def step(j6, e, third, last=False, next_gather=True):
                    take_y(es, e + 1)
                    if not last:
                        silu(es, e + 2)
                    if j6 % 3 == 2 and next_gather:
                        odd_fills((j6 // 3) % 2, third + 2)

                with act.Fori(0, 4) as it:
                    for j6 in range(6):
                        step(j6, it * 6 + j6, it * 2 + j6 // 3)
                for e in range(24, NE):
                    step(e % 6, e, e // 3, last=(e == NE - 1), next_gather=(e // 3 < 9))
                most = act.value_load(busiest_i[0:1, 0:1], min_val=0, max_val=S)
                with act.If(most > CAP):
                    with act.Fori(0, ROUNDS - 1) as r:
                        with act.Fori(0, NE) as e:
                            silu(xs, r * NE + e + 1)
                            take_y(xs, r * NE + e + 1)
                act.wait_ge(acc_done, l + 1)
                for nh in range(2):
                    last = nc.scalar.copy(H[:, 1, nh * 512:(nh + 1) * 512], PS[:, 2 + nh, :])
                last.then_inc(moe_act, 1)
                act.wait_ge(moe_act, l + 1)
                act.wait_ge(moe_dve, l + 1)

            act.wait_ge(mixed, 4)
            norm(1)
            expert_layer(0)
            norm(2)
            act.wait_ge(lam_dot, 1)
            af(lams[:, 2:4], lams[:, 0:2], ACT.Exp).then_inc(lam_exp, 1)
            for b in range(4):
                act.wait_ge(kproj_psum, b + 1)
                nc.scalar.copy(KT[:, 2 * b:2 * b + 2, :], PS[:, b, :].rearrange("p (a t) -> p a t", a=2)).then_inc(kproj_ready, 1)
            for nh in range(2):
                for t in range(TB):
                    act.wait_ge(vb_psum, 2 * nh + t + 1)
                    nc.scalar.copy(XN[:, t, nh * 512:(nh + 1) * 512], PS[:, 4 + 2 * nh + t, :]).then_inc(vb_ready, 1)
            for b in range(4):
                act.wait_ge(qproj_psum, b + 1)
                nc.scalar.copy(QT[:, 2 * b:2 * b + 2, :], PS[:, b, :].rearrange("p (a t) -> p a t", a=2)).then_inc(qproj_ready, 1)

            def exps(h):
                act.wait_ge(s_max, 2 * (h + 1))
                a = att_s[:, h % 3, :]
                for m in range(2):
                    for b, c in ((0, slice(0, P)), (1, slice(P, 3 * P))):
                        i = 2 * m + b
                        v = SM[:, h % 3, m, c]
                        last = af(v, v, ACT.Exp, bias=a[:, 4 + i:5 + i], accum_out=a[:, 8 + i:9 + i])
                last.then_inc(s_exp, 1)

            def turned_probs(h):
                act.wait_ge(pt_psum, h + 1)
                if h >= 2:
                    act.wait_ge(ob_psum, h - 1)
                nc.scalar.copy(PT[:, h % 2, :], PS[:, h % 2, 0:3 * P]).then_inc(pt_ready, 1)

            def outputs(h):
                act.wait_ge(ob_psum, h + 1)
                for b in range(TB):
                    af(OB[:, b, h * P:(h + 1) * P], PS[:, 2 + h % 2, b * P:(b + 1) * P], ACT.Square,
                       accum_out=hsum[:, b * HEADS + h:b * HEADS + h + 1]).then_inc(act_own, 1)
                own.n += TB
                act.wait_ge(act_own, own.n)
                nc.scalar.copy(OB[:, :, h * P:(h + 1) * P],
                               PS[:, 2 + h % 2, 0:S].rearrange("p (b c) -> p b c", b=TB)).then_inc(ob_ready, 1)

            for i in range(HEADS + 2):
                if i < HEADS:
                    exps(i)
                if 1 <= i <= HEADS:
                    turned_probs(i - 1)
                if i >= 2:
                    outputs(i - 2)
            turned_heads(1, sub_gain[:, 0:1], range(4))
            act.wait_ge(mixed, 8)
            norm(3)
            expert_layer(1)
            norm(4, turn=False)
            act.wait_ge(xn1_ready, 5)
            act.wait_ge(final_gain_landed, 16)

        @block.vector
        def _(dve):
            own = Chain(dve, dve_own)
            vt, vs, stt, red = nc.vector.tensor_tensor, nc.vector.tensor_scalar, nc.vector.scalar_tensor_tensor, nc.vector.tensor_reduce

            def norm(i, turn=True):
                dve.wait_ge(squares, 2 * (i + 1))
                vs(ssum[:], ssum[:], 1.0 / D, 1e-6, ALU.mult, ALU.add).then_inc(variances, 1)
                dve.wait_ge(rstd_ready, i + 1)
                dst = XN[:, 0, :] if turn else OUTB[:, 0, :]
                vs(dst, H[:, 0, :], rstd[:, 0:1], None, ALU.mult).then_inc(xn0_ready, 1)
                if not turn:
                    return
                for b in (0, 1):
                    dve.wait_ge(xt_psum, 4 * i + b + 1)
                    for j in range(2):
                        k = 2 * b + j
                        g = {0: GA_A, 1: GA_F, 2: GA_KV, 3: GA_F + 8}[i]
                        if i == 2:
                            own.link(vs(XT2[:, k, :], PS[:, 4 + b, j * S:(j + 1) * S], gains[:, GA_B + k:GA_B + k + 1], None, ALU.mult))
                        vs(XT[:, k, :], PS[:, 4 + b, j * S:(j + 1) * S], gains[:, g + k:g + k + 1], None,
                           ALU.mult).then_inc(xt_dve, 1)

            dve.wait_ge(gains_psum, 1)
            nc.vector.tensor_copy(gains[:], PS[:, 0, 0:NG]).then_inc(gains_ready, 1)
            dve.wait_ge(gains_ready, 1)
            l0, l1 = gains[:, GA_LB:GA_LB + 8], gains[:, GA_LB + 8:GA_LB + 16]
            own.link(vs(sub_gain[:], gains[:, GA_SL:GA_SL + 1], 1.0 - LAM_INIT, None, ALU.mult))
            own.link(vt(lbt[:, 2, :], l0, l1, ALU.max))
            own.link(vt(lbt[:, 0, :], l0, lbt[:, 2, :], ALU.subtract))
            vt(lbt[:, 1, :], l1, lbt[:, 2, :], ALU.subtract).then_inc(lb_max, 1)
            norm(0)
            dve.wait_ge(lb_exp, 1)
            own.link(vt(lbt[:, 2, :], lbt[:, 0, :], lbt[:, 1, :], ALU.add))
            own.link(nc.vector.reciprocal(lbt[:, 2, :], lbt[:, 2, :]))
            own.link(vt(lbt[:, 3, :], lbt[:, 0, :], lbt[:, 2, :], ALU.mult))
            own.link(vs(lbt[:, 4, :], lbt[:, 3, :], -1.0, 1.0, ALU.mult, ALU.add))
            for h in range(HEADS):
                dve.wait_ge(qf_sig, h + 1)
                c = slice(h * S, (h + 1) * S)
                vt(QD[:, h, :], QD[:, h, :], PS[:, h % 4, 0:S], ALU.mult).then_inc(qf_free, 1)
                vs(KF[:, c], KF[:, c], lbt[:, 4, h:h + 1], None, ALU.mult)
                vs(BC[:, c], BC[:, c], lbt[:, 4, h:h + 1], lbt[:, 3, h:h + 1], ALU.mult, ALU.add).then_inc(qf_lin, 1)
            for hf in range(2):
                dve.wait_ge(logf_ready, hf + 1)
                for d in range(5):
                    w = 1 << d
                    v = BC[:, hf * 1024:(hf + 1) * 1024].rearrange("p (g two w) -> p g two w", two=2, w=w)
                    op = vt(v[:, :, 1, :], v[:, :, 1, :], v[:, :, 0, w - 1:w].to_broadcast([P, 1024 // (2 * w), w]), ALU.add)
                    if d < 4:
                        own.link(op)
                    else:
                        op.then_inc(cum_ready, 1)
            for hf in range(2):
                dve.wait_ge(exps_ready, hf + 1)
                c = slice(hf * 1024, (hf + 1) * 1024)
                last_of = EX[:, c].rearrange("p (g w) -> p g w", w=CH)[:, :, CH - 1]
                nc.vector.tensor_copy(chunk_decay[:, 4 * hf:4 * hf + 4, :].rearrange("p h n -> p (h n)"), last_of)
                vt(WK1[:, c], WK1[:, c], EX[:, c], ALU.mult)
                own.link(vt(WK2[:, c], WK2[:, c], KF[:, c], ALU.mult))
                v = BC[:, c].rearrange("p (g w) -> p g w", w=CH)
                lastb = lbt_last[:, hf, :]
                own.link(nc.vector.tensor_copy(lastb, v[:, :, CH - 1]))
                vt(v, lastb.unsqueeze(2).to_broadcast([P, 32, CH]), v, ALU.subtract).then_inc(rest_ready, 1)
            for hf in range(2):
                dve.wait_ge(rest_exp, hf + 1)
                c = slice(hf * 1024, (hf + 1) * 1024)
                vt(KF[:, c], KF[:, c], EX[:, c], ALU.mult).then_inc(kend_ready, 1)
            for nh in range(2):
                for t in range(TB):
                    dve.wait_ge(g_sig, 2 * nh + t + 1)
                    v = GATE[:, t, nh * 512:(nh + 1) * 512]
                    vt(v, v, PS[:, 2 * nh + t, :], ALU.mult).then_inc(gate_ready, 1)
            dve.wait_ge(masked_zero, 1)
            dve.wait_ge(consts_ready, 6)
            SC = EX.rearrange("p (h t) -> p h t", h=HEADS)
            for h in range(HEADS):
                dve.wait_ge(score_psum, h + 1)
                nc.vector.copy_predicated(SC[:, h, :].rearrange("p (b c) -> p b c", b=TB),
                                          chunk_mask[:].unsqueeze(1).to_broadcast([P, TB, P]),
                                          PS[:, 4 + h % 4, 0:S].rearrange("p (b c) -> p b c", b=TB)).then_inc(score_ready, 1)
            for i, (t, hh) in enumerate(((0, 0), (0, 1), (1, 0), (1, 1))):
                dve.wait_ge(kv_psum, i + 1)
                if i >= 2:
                    dve.wait_ge(o_psum, i - 1)
                for c in range(4 - t):
                    n = 4 * t + c
                    for h in range(4):
                        kvp = PS[:, 4 + c, h * P:(h + 1) * P]
                        dst = ST[hh][:, (n + 1) % 4, h * P:(h + 1) * P]
                        if n == 0:
                            last = nc.vector.tensor_copy(dst, kvp)
                        else:
                            last = stt(out=dst, in0=ST[hh][:, n % 4, h * P:(h + 1) * P],
                                       scalar=chunk_decay[:, 4 * hh + h, n:n + 1], in1=kvp, op0=ALU.mult, op1=ALU.add)
                    if c < 3 - t:
                        own.link(last)
                last.then_inc(state_ready, 1)
                dve.wait_ge(state_ready, i + 1)
            O = BC.rearrange("p (b f) -> p b f", b=TB)
            for b in range(4):
                dve.wait_ge(o_sq, b + 1)
                own.link(red(hsum[:, 4 * b:4 * b + 4], BC[:, b * 512:(b + 1) * 512].rearrange("p (h v) -> p h v", v=P),
                             AX, ALU.add))
            vs(hsum[:], hsum[:], 1.0 / P, 1e-6, ALU.mult, ALU.add).then_inc(o_var, 1)
            dve.wait_ge(o_rstd, 1)
            for b in range(4):
                v = BC[:, b * 512:(b + 1) * 512].rearrange("p (h v) -> p h v", v=P)
                own.link(vt(v, PS[:, b, :].rearrange("p (h v) -> p h v", v=P),
                            hrstd[:, 4 * b:4 * b + 4].unsqueeze(2).to_broadcast([P, 4, P]), ALU.mult))
            vt(BC, BC, WK4[:, :], ALU.mult).then_inc(o_ready, 1)

            def add_mix(i):
                for t in range(TB):
                    for nh in range(2):
                        dve.wait_ge(mix_psum, 4 * i + 2 * t + nh + 1)
                        v = H[:, t, nh * 512:(nh + 1) * 512]
                        vt(v, v, PS[:, 2 * t + nh, :], ALU.add).then_inc(mixed, 1)
                dve.wait_ge(mixed, 4 * (i + 1))

            add_mix(0)
            norm(1)

            def expert_layer(l):
                es, xs = main_s[l], more_s[l]
                R = lambda i, w=8: rt[:, i, :, 0:w]
                wide_ = lambda a, w: a.to_broadcast([P, TB, w])

                def first_max(src, w, r_max, r_tmp, r_hot):
                    own.link(red(R(r_max, 1), src, AX, ALU.max))
                    own.link(vt(R(r_tmp, w), src, wide_(R(r_max, 1), w), ALU.is_equal))
                    own.link(stt(out=R(r_tmp, w), in0=R(r_tmp, w), scalar=-100.0,
                                 in1=slot_iota[:, 0:w].unsqueeze(1).to_broadcast([P, TB, w]), op0=ALU.mult, op1=ALU.add))
                    own.link(red(R(r_hot, 1), R(r_tmp, w), AX, ALU.min))
                    own.link(nc.vector.tensor_copy(R(15, 1), R(r_hot, 1)))
                    own.link(vt(R(r_hot, w), R(r_tmp, w), wide_(R(15, 1), w), ALU.is_equal))

                dve.wait_ge(logits_psum, l + 1)
                own.link(vt(logit, PS[:, B_XG, 0:TB * LG].rearrange("p (t n) -> p t n", t=TB),
                            rb[:, l, :].unsqueeze(1).to_broadcast([P, TB, LG]), ALU.add))
                first_max(logit[:, :, 0:G4], G4, 2, 3, 4)
                vt(R(0, G4), logit[:, :, 0:G4], wide_(R(2, 1), G4), ALU.subtract).then_inc(coarse_in, 1)
                own.link(vt(rt4, logit[:, :, G4:LG].rearrange("p t (g j) -> p t g j", g=G4),
                            R(4, G4).unsqueeze(3).to_broadcast([P, TB, G4, E8]), ALU.mult))
                own.link(red(R(5), rt4.rearrange("p t g j -> p t j g"), AX, ALU.add))
                first_max(R(5), E8, 6, 3, 7)
                own.link(stt(out=R(10), in0=R(7), scalar=NEG, in1=R(5), op0=ALU.mult, op1=ALU.add))
                first_max(R(10), E8, 11, 3, 12)
                vt(R(8, 1), R(11, 1), R(6, 1), ALU.subtract).then_inc(fine_in, 1)
                dve.wait_ge(coarse_exp, l + 1)
                own.link(red(R(2, 1), R(1, G4), AX, ALU.add))
                own.link(nc.vector.reciprocal(R(2, 1), R(2, 1)))
                dve.wait_ge(fine_exp, l + 1)
                own.link(vs(R(3, 1), R(9, 1), 1.0, None, ALU.add))
                own.link(nc.vector.reciprocal(R(3, 1), R(3, 1)))
                own.link(vt(R(13, 1), R(2, 1), R(3, 1), ALU.mult))
                own.link(vt(R(14, 1), R(13, 1), R(9, 1), ALU.mult))
                own.link(vt(R(0), R(7), R(12), ALU.add))
                own.link(vt(R(1), R(7), wide_(R(13, 1), E8), ALU.mult))
                own.link(vt(R(5), R(12), wide_(R(14, 1), E8), ALU.mult))
                own.link(vt(R(1), R(1), R(5), ALU.add))
                grp = R(4, G4).unsqueeze(3).to_broadcast([P, TB, G4, E8])
                own.link(vt(gate[:, :, 0:NE].rearrange("p t (g j) -> p t g j", g=G4), grp,
                            R(1).unsqueeze(2).to_broadcast([P, TB, G4, E8]), ALU.mult))
                own.link(nc.vector.memset(gate[:, :, NE:SW], 0.0))
                own.link(nc.vector.memset(slot[:, :, NE:SW], FAR))
                vt(member.rearrange("p t (g j) -> p t g j", g=G4), grp,
                   R(0).unsqueeze(2).to_broadcast([P, TB, G4, E8]), ALU.mult).then_inc(member_ready, 1)
                dve.wait_ge(member_ready, l + 1)
                own.link(vs(slot[:, :, 0:NE], member, -FAR, FAR, ALU.mult, ALU.add))
                dve.wait_ge(ranks_psum, l + 1)
                own.link(vt(slot[:, :, 0:NE], slot[:, :, 0:NE], PS[:, B_XG, 0:2 * NE].rearrange("p (t n) -> p t n", t=TB), ALU.add))
                own.link(red(busiest[:, 0:1], PS[:, B_XG, 2 * NE:3 * NE], AX, ALU.max))
                nc.vector.tensor_copy(busiest_i[:], busiest[:, 0:1]).then_inc(slots_ready, 1)

                def even_fills(buf, group):
                    for q in (0, 2):
                        dve.wait_ge(es.gathered, group * 4 + (q + 1))
                        for j in range(2):
                            k = 2 * q + j
                            last = vs(XE[buf][:, k, :], PS[:, B_XG, j * GRP * CAP:(j + 1) * GRP * CAP],
                                      gains[:, GA_F + 8 * l + k:GA_F + 8 * l + k + 1], None, ALU.mult)
                        last.then_inc(es.even_taken, 1)

                def build_dispatch(es_, buf, e, n):
                    nc.vector.tensor_tensor(PD[:, buf, :, 0:n, :],
                                            slot[:, :, bass.ds(e, n)].unsqueeze(3).to_broadcast([P, TB, n, CAP]),
                                            slot_iota[:].unsqueeze(1).unsqueeze(1).to_broadcast([P, TB, n, CAP]),
                                            ALU.is_equal).then_inc(es_.dispatch_built, 1)

                def times_up(es_, count):
                    dve.wait_ge(es_.silu_done, count)
                    vt(HH, HS, PS[:, B_GU, S:2 * S], ALU.mult).then_inc(es_.act_done, 1)

                def take_turned(es_, count):
                    dve.wait_ge(es_.turned, count)
                    nc.vector.tensor_copy(HG[:, 0:S], PS[:, B_TR, 0:S]).then_inc(es_.turned_taken, 1)
                    nc.vector.tensor_copy(HG[:, S:2 * S], PS[:, B_TR, S:2 * S]).then_inc(es_.turned_taken, 1)

                dve.wait_ge(slots_ready, l + 1)
                dve.wait_ge(part_made, 3 * (l + 1))
                build_dispatch(es, 0, 0, GRP)
                build_dispatch(es, 1, GRP, GRP)
                even_fills(0, 0)
                times_up(es, 1)
                even_fills(1, 1)

                def step(j6, e, third, last=False, next_gather=True, next_tables=True):
                    take_turned(es, e + 1)
                    if not last:
                        times_up(es, e + 2)
                    if j6 % 3 == 2 and next_gather:
                        even_fills((j6 // 3) % 2, third + 2)
                    if j6 % 3 == 0 and next_tables:
                        dve.wait_ge(es.gates_built, third * 4 + 4)
                        build_dispatch(es, (j6 // 3) % 2, e + 6, GRP)

                with dve.Fori(0, 4) as it:
                    for j6 in range(6):
                        step(j6, it * 6 + j6, it * 2 + j6 // 3)
                for e in range(24, NE):
                    step(e % 6, e, e // 3, last=(e == NE - 1), next_gather=(e // 3 < 9), next_tables=(e == 24))
                most = dve.value_load(busiest_i[0:1, 0:1], min_val=0, max_val=S)
                with dve.If(most > CAP):
                    with dve.Fori(0, ROUNDS - 1) as r:
                        dve.wait_ge(xs.combined, r * NE + 1)
                        vs(slot, slot, float(CAP), None, ALU.subtract).then_inc(more_shift[l], 1)
                        with dve.Fori(0, NE) as e:
                            n = r * NE + e
                            dve.wait_ge(more_shift[l], r + 1)
                            dve.wait_ge(xs.combined, n + 1)
                            build_dispatch(xs, 0, e, 1)
                            dve.wait_ge(xs.gathered, n + 1)
                            for k in range(KC):
                                last = vs(XE[0][:, k, 0:CAP], PS[:, B_XG, k * CAP:(k + 1) * CAP],
                                          gains[:, GA_F + 8 * l + k:GA_F + 8 * l + k + 1], None, ALU.mult)
                            last.then_inc(xs.even_taken, 1)
                            times_up(xs, n + 1)
                            take_turned(xs, n + 1)
                dve.wait_ge(acc_done, l + 1)
                for nh in range(2):
                    last = nc.vector.tensor_copy(H[:, 0, nh * 512:(nh + 1) * 512], PS[:, nh, :])
                last.then_inc(moe_dve, 1)

            expert_layer(0)
            norm(2)
            lv = lam[:].rearrange("p (a b) d -> p a b d", b=2)
            own.link(vt(lamt, lv[:, :, 0, :], lv[:, :, 1, :], ALU.mult))
            red(lams[:, 0:2], lamt, AX, ALU.add).then_inc(lam_dot, 1)
            dve.wait_ge(lam_exp, 1)
            own.link(vt(lams[:, 4:5], lams[:, 3:4], lams[:, 2:3], ALU.subtract))
            own.link(vs(lams[:, 5:6], lams[:, 4:5], -LAM_INIT, None, ALU.add))

            def masked(h):
                dve.wait_ge(s_psum, h + 1)
                if h >= 3:
                    dve.wait_ge(pt_psum, h - 2)
                a = att_s[:, h % 3, :]
                for m in range(2):
                    own.link(stt(out=SM[:, h % 3, m, :], in0=PS[:, 4 + 2 * (h % 2) + m, 0:3 * P], scalar=DH ** -0.5,
                                 in1=causal_neg, op0=ALU.mult, op1=ALU.add))
                for m in range(2):
                    red(a[:, 2 * m:2 * m + 1], SM[:, h % 3, m, 0:P], AX, ALU.max)
                    op = red(a[:, 2 * m + 1:2 * m + 2], SM[:, h % 3, m, P:3 * P], AX, ALU.max)
                    own.link(op)
                    vs(a[:, 4 + 2 * m:6 + 2 * m], a[:, 2 * m:2 * m + 2], -1.0, None, ALU.mult).then_inc(s_max, 1)

            def mixed_probs(h):
                dve.wait_ge(s_exp, h + 1)
                a = att_s[:, h % 3, :]
                own.link(nc.vector.reciprocal(a[:, 12:16], a[:, 8:12]))
                own.link(vs(a[:, 14:16], a[:, 14:16], lams[:, 5:6], None, ALU.mult))
                for b, c in ((0, slice(0, P)), (1, slice(P, 3 * P))):
                    own.link(vs(SM[:, h % 3, 0, c], SM[:, h % 3, 0, c], a[:, 12 + b:13 + b], None, ALU.mult))
                    op = stt(out=SM[:, h % 3, 0, c], in0=SM[:, h % 3, 1, c], scalar=a[:, 14 + b:15 + b],
                             in1=SM[:, h % 3, 0, c], op0=ALU.mult, op1=ALU.add)
                op.then_inc(p_ready, 1)

            dve.wait_ge(causal_ready, 2)
            masked(0)
            for h in range(1, HEADS):
                masked(h)
                mixed_probs(h - 1)
            mixed_probs(HEADS - 1)
            dve.wait_ge(ob_ready, HEADS)
            vs(hsum[:], hsum[:], 1.0 / P, 1e-5, ALU.mult, ALU.add).then_inc(o_var, 1)
            dve.wait_ge(o_rstd, 2)
            v = WK4[:, :].rearrange("p (g v) -> p g v", v=P)
            vt(v, v, hrstd[:].unsqueeze(2).to_broadcast([P, 16, P]), ALU.mult).then_inc(o_ready, 1)
            add_mix(1)
            norm(3)
            expert_layer(1)
            norm(4, turn=False)
            dve.wait_ge(final_gain_landed, 16)
            dve.wait_ge(xn0_ready, 5)
            vt(OUTB[:, 0, :], OUTB[:, 0, :], GROW, ALU.mult).then_inc(final_dve, 1)
            dve.wait_ge(xn1_ready, 5)
            vt(OUTB[:, 1, :], OUTB[:, 1, :], GROW, ALU.mult).then_inc(final_act, 1)


_INS = ["x", "a_norm_g", "a_w_in", "a_lb", "a_onorm_g", "a_w_out", "kv_norm_g", "w_kv", "b_norm_g", "b_w_q",
        "b_lam", "b_subln_g", "b_w_out", "ffn_norm_g", "router_g_w", "router_g_b", "router_e_w", "router_e_b",
        "expert_w_gu", "expert_w_down", "final_norm_g"]


def kernel(**inputs):
    import numpy as _np
    import concourse.bacc as _bacc
    from concourse.bass_utils import run_bass_kernel_spmd as _run

    nc = _bacc.Bacc("TRN2", target_bir_lowering=False, num_devices=1)
    arrays, args = {}, []
    for name in _INS:
        a = _np.ascontiguousarray(inputs[name])
        arrays[f"in_{name}_dram"] = a
        args.append(nc.dram_tensor(f"in_{name}_dram", a.shape, mybir.dt.from_np(a.dtype), kind="ExternalInput").ap())
    args.append(nc.dram_tensor("out_dram", (1, S, D), F32, kind="ExternalOutput").ap())
    trunk(nc, *args)
    r = _run(nc, [arrays], core_ids=[0])
    return r.results[0]["out_dram"]
```
